# Optimizing a Trainium2 kernel written in Bass

```python
import math
import jax, jax.numpy as jnp
from jax import lax
import numpy as np

D_MODEL = 1024
BATCH = 1
SEQ = 1024
DEPTH = 1

HEAD_DIM_A = 128
KV_HEADS_A = 4
DILATED_GROUPS = ((128, 1), (512, 4), (2048, 16))
N_GROUPS_A = len(DILATED_GROUPS)
Q_HEADS_A = KV_HEADS_A * N_GROUPS_A
ROPE_THETA = 10000.0
GLA_HEADS = 4
GLA_DK = D_MODEL // 2 // GLA_HEADS
GLA_DV = D_MODEL // GLA_HEADS
GLA_LOWRANK = 16
GLA_GATE_TEMP = 16.0
GLA_CHUNK = 64
D_FF = -(-8 * D_MODEL // (3 * 256)) * 256
EPS = 1e-6

W_QA = Q_HEADS_A * HEAD_DIM_A
W_KA = KV_HEADS_A * HEAD_DIM_A
W_VA = KV_HEADS_A * HEAD_DIM_A
W_QB = GLA_HEADS * GLA_DK
W_KB = GLA_HEADS * GLA_DK
W_VB = GLA_HEADS * GLA_DV
W_RB = GLA_HEADS * GLA_DV
IN_SPLITS = (W_QA, W_KA, W_VA, W_QB, W_KB, W_VB, W_RB, GLA_LOWRANK, D_MODEL, D_MODEL)
D_IN = sum(IN_SPLITS)
D_OUT_A = W_VA
D_OUT_B = W_VB

kernel_name = "hybrid_dilated_attn_gla_swiglu"

def rmsnorm(x, g):
    xf = x.astype(jnp.float32)
    y = xf * lax.rsqrt(jnp.mean(xf * xf, axis=-1, keepdims=True) + EPS) * g.astype(jnp.float32)
    return y.astype(x.dtype)

def rope_tables(positions):
    inv_freq = ROPE_THETA ** (-jnp.arange(0, HEAD_DIM_A, 2, dtype=jnp.float32) / HEAD_DIM_A)
    ang = positions.astype(jnp.float32)[..., None] * inv_freq
    return jnp.cos(ang)[:, :, None, :], jnp.sin(ang)[:, :, None, :]

def apply_rope(t, cos, sin):
    tf = t.astype(jnp.float32)
    t1, t2 = jnp.split(tf, 2, axis=-1)
    return jnp.concatenate([t1 * cos - t2 * sin, t2 * cos + t1 * sin], axis=-1).astype(t.dtype)

def dilated_group(q, k, v, window, dilation):
    B, S, H, hd = q.shape
    nk = window // dilation
    L = S // dilation
    nb = -(-L // nk)
    Lp = nb * nk

    def to_blocks(t):
        t = t.astype(jnp.float32).reshape(B, L, dilation, H, hd).transpose(0, 2, 3, 1, 4)
        t = jnp.pad(t, ((0, 0), (0, 0), (0, 0), (0, Lp - L), (0, 0)))
        return t.reshape(B, dilation, H, nb, nk, hd)

    def with_prev(t):
        prev = jnp.pad(t, ((0, 0), (0, 0), (0, 0), (1, 0), (0, 0), (0, 0)))[:, :, :, :-1]
        return jnp.concatenate([prev, t], axis=4)

    qb = to_blocks(q)
    kb = with_prev(to_blocks(k))
    vb = with_prev(to_blocks(v))
    s = jnp.einsum('brhnqe,brhnke->brhnqk', qb, kb)
    qi = jnp.arange(nk)[:, None] + nk
    ki = jnp.arange(2 * nk)[None, :]
    dist = qi - ki
    blk = jnp.arange(nb)[:, None, None]
    valid = (dist >= 0) & (dist <= nk) & (blk * nk + ki - nk >= 0)
    s = jnp.where(valid, s, -jnp.inf)
    m = jnp.max(s, axis=-1, keepdims=True)
    p = jnp.exp(s - m)
    den = jnp.sum(p, axis=-1)
    o = jnp.einsum('brhnqk,brhnke->brhnqe', p, vb) / den[..., None]
    lse = m[..., 0] + jnp.log(den)
    o = o.reshape(B, dilation, H, Lp, hd)[:, :, :, :L].transpose(0, 3, 1, 2, 4).reshape(B, S, H, hd)
    lse = lse.reshape(B, dilation, H, Lp)[:, :, :, :L].transpose(0, 3, 1, 2).reshape(B, S, H)
    return o, lse

def dilated_attention(q, k, v):
    outs, lses = [], []
    for g, (window, dilation) in enumerate(DILATED_GROUPS):
        o, lse = dilated_group(q[:, :, g], k, v, window, dilation)
        outs.append(o)
        lses.append(lse)
    w = jax.nn.softmax(jnp.stack(lses, axis=0), axis=0)
    o = jnp.sum(w[..., None] * jnp.stack(outs, axis=0), axis=0)
    return o.astype(v.dtype)

def gla(q, k, v, log_a):
    B, S, H, dk = q.shape
    dv = v.shape[-1]
    nc = S // GLA_CHUNK

    def to_chunks(t):
        return t.astype(jnp.float32).reshape(B, nc, GLA_CHUNK, H, -1).transpose(1, 0, 3, 2, 4)

    qc, kc, vc = to_chunks(q), to_chunks(k), to_chunks(v)
    bc = jnp.cumsum(to_chunks(log_a), axis=3)
    causal = jnp.tril(jnp.ones((GLA_CHUNK, GLA_CHUNK), dtype=bool))[:, :, None]

    def step(state, xs):
        qi, ki, vi, bi = xs
        b_last = bi[:, :, -1:, :]
        inter = jnp.einsum('bhtd,bhde->bhte', qi * jnp.exp(bi), state)
        diff = bi[:, :, :, None, :] - bi[:, :, None, :, :]
        decay = jnp.exp(jnp.where(causal, diff, -jnp.inf))
        att = jnp.einsum('bhtd,bhsd,bhtsd->bhts', qi, ki, decay)
        intra = jnp.einsum('bhts,bhse->bhte', att, vi)
        new_state = jnp.exp(b_last[:, :, 0, :])[..., None] * state + jnp.einsum(
            'bhsd,bhse->bhde', ki * jnp.exp(b_last - bi), vi)
        return new_state, inter + intra

    state0 = jnp.zeros((B, H, dk, dv), jnp.float32)
    _, o = lax.scan(step, state0, (qc, kc, vc, bc))
    return o.transpose(1, 0, 3, 2, 4).reshape(B, S, H, dv).astype(v.dtype)

def hybrid_layer(x, cos, sin, norm1, w_in, qn_a, kn_a, w_a_up, b_a, gn_b,
                 w_proj_a, w_proj_b, w_out, norm2, w_ffn_gate, w_ffn_up, w_ffn_down):
    B, S, _ = x.shape
    h = rmsnorm(x, norm1)
    proj = h @ w_in
    offsets = np.cumsum(IN_SPLITS)[:-1].tolist()
    qa, ka, va, qb, kb, vb, rb, ab, ga, gb = jnp.split(proj, offsets, axis=-1)

    qa = apply_rope(rmsnorm(qa.reshape(B, S, Q_HEADS_A, HEAD_DIM_A), qn_a), cos, sin) * (HEAD_DIM_A ** -0.5)
    ka = apply_rope(rmsnorm(ka.reshape(B, S, KV_HEADS_A, HEAD_DIM_A), kn_a), cos, sin)
    va = va.reshape(B, S, KV_HEADS_A, HEAD_DIM_A)
    oa = dilated_attention(qa.reshape(B, S, N_GROUPS_A, KV_HEADS_A, HEAD_DIM_A), ka, va)
    oa = oa.reshape(B, S, D_OUT_A)

    qb = qb.reshape(B, S, GLA_HEADS, GLA_DK) * (GLA_DK ** -0.5)
    kb = kb.reshape(B, S, GLA_HEADS, GLA_DK)
    vb = vb.reshape(B, S, GLA_HEADS, GLA_DV)
    log_a = jax.nn.log_sigmoid((ab @ w_a_up + b_a).astype(jnp.float32)) / GLA_GATE_TEMP
    ob = gla(qb, kb, vb, log_a.reshape(B, S, GLA_HEADS, GLA_DK))
    ob = rmsnorm(ob, gn_b) * jax.nn.silu(rb.reshape(B, S, GLA_HEADS, GLA_DV))
    ob = ob.reshape(B, S, D_OUT_B)

    y = jax.nn.sigmoid(ga) * (oa @ w_proj_a) + jax.nn.sigmoid(gb) * (ob @ w_proj_b)
    x = x + y @ w_out

    h2 = rmsnorm(x, norm2)
    x = x + (jax.nn.silu(h2 @ w_ffn_gate) * (h2 @ w_ffn_up)) @ w_ffn_down
    return x

def setup_inputs(seed: int = 0) -> dict:
    key = jax.random.key(seed)
    ks = jax.random.split(key, 20)
    f32 = jnp.float32

    def nrm(k, shape, scale):
        return jax.random.normal(k, shape, f32) * scale

    L = DEPTH
    return {
        "x": jax.random.normal(ks[0], (BATCH, SEQ, D_MODEL), f32),
        "positions": jax.random.randint(ks[1], (BATCH, 1), 0, 4096, dtype=jnp.int32)
                     + jnp.arange(SEQ, dtype=jnp.int32)[None, :],
        "norm1": 1.0 + nrm(ks[2], (L, D_MODEL), 0.05),
        "w_in": nrm(ks[3], (L, D_MODEL, D_IN), D_MODEL ** -0.5),
        "qn_a": 1.0 + nrm(ks[4], (L, HEAD_DIM_A), 0.05),
        "kn_a": 1.0 + nrm(ks[5], (L, HEAD_DIM_A), 0.05),
        "w_a_up": nrm(ks[6], (L, GLA_LOWRANK, W_KB), GLA_LOWRANK ** -0.5),
        "b_a": nrm(ks[7], (L, W_KB), 0.1),
        "gn_b": 1.0 + nrm(ks[8], (L, GLA_DV), 0.05),
        "w_proj_a": nrm(ks[9], (L, D_OUT_A, D_MODEL), D_OUT_A ** -0.5),
        "w_proj_b": nrm(ks[10], (L, D_OUT_B, D_MODEL), D_OUT_B ** -0.5),
        "w_out": nrm(ks[11], (L, D_MODEL, D_MODEL), 0.5 * D_MODEL ** -0.5),
        "norm2": 1.0 + nrm(ks[12], (L, D_MODEL), 0.05),
        "w_ffn_gate": nrm(ks[13], (L, D_MODEL, D_FF), D_MODEL ** -0.5),
        "w_ffn_up": nrm(ks[14], (L, D_MODEL, D_FF), D_MODEL ** -0.5),
        "w_ffn_down": nrm(ks[15], (L, D_FF, D_MODEL), 0.5 * D_FF ** -0.5),
    }

def reference(x, positions, norm1, w_in, qn_a, kn_a, w_a_up, b_a, gn_b, w_proj_a, w_proj_b,
              w_out, norm2, w_ffn_gate, w_ffn_up, w_ffn_down):
    cos, sin = rope_tables(positions)
    for l in range(DEPTH):
        x = hybrid_layer(x, cos, sin, norm1[l], w_in[l], qn_a[l], kn_a[l], w_a_up[l], b_a[l], gn_b[l],
                         w_proj_a[l], w_proj_b[l], w_out[l], norm2[l], w_ffn_gate[l], w_ffn_up[l],
                         w_ffn_down[l])
    return x


_drawn_inputs = setup_inputs


def setup_inputs(seed=0):
    import zlib

    import numpy as np

    out = dict(_drawn_inputs(seed))
    spreads = {}
    factors = {'norm1': 3.051,
     'qn_a': 8.0,
     'kn_a': 8.0,
     'w_a_up': 3.306,
     'b_a': 7.563,
     'gn_b': 7.083,
     'norm2': 2.828}
    for name, (base, spread) in spreads.items():
        noise = np.random.default_rng([zlib.crc32(name.encode()), seed]).standard_normal(out[name].shape)
        drawn = base * np.exp(spread * noise) if base else spread * noise
        out[name] = __import__('jax').numpy.asarray(drawn.astype(out[name].dtype))
    for name, factor in factors.items():
        out[name] = (out[name] * factor).astype(out[name].dtype)
    return out
```

```python
from contextlib import ExitStack

import concourse.bass as bass
from concourse import mybir

F32 = mybir.dt.float32
F32R = mybir.dt.float32r
I32 = mybir.dt.int32
ALU = mybir.AluOpType
ACT = mybir.ActivationFunctionType
AX = mybir.AxisListType

P = 128
HALF = 512
NEG = -1.0e30
TWO_PI = 6.283185307179586
ROUND = 12582912.0
PI_C1 = 6.28125
PI_C2 = 0.0019340515136718750
PI_C3 = TWO_PI - PI_C1 - PI_C2
PI_SAFE = 3.1415925


def decoder_layer(nc, x_d, pos_d, norm1_d, w_in_d, qn_d, kn_d, w_up_d, b_a_d, gn_d, w_pa_d, w_pb_d,
                  w_out_d, norm2_d, w_fg_d, w_fu_d, w_fd_d, inv_freq_d, out_d):
    S, D = x_d.shape[1], x_d.shape[2]
    NT = S // P
    NK = D // P
    FF = w_fg_d.shape[2]
    LR = w_up_d.shape[1]
    H = 4
    NG = 3
    DV = gn_d.shape[1]
    W_Q, W_KV, W_B = NG * H * P, H * P, H * P
    C_K = W_Q
    C_V = C_K + W_KV
    C_QB = C_V + W_KV
    C_KB = C_QB + W_B
    C_VB = C_KB + W_B
    C_RB = C_VB + H * DV
    C_AB = C_RB + H * DV
    C_G = C_AB + LR
    SCALE = float(P) ** -0.5
    EPS = 1e-6
    TEMP = 16.0
    assert S == 1024 and D == 1024 and DV == 256 and C_G + 2 * D == w_in_d.shape[2]

    TA, TB, TC = 9, 6, 6
    A0, B0, C0 = 0, H * TA, H * (TA + TB)
    NC_IT = D // (2 * P)
    D0 = C0 + NC_IT * TC
    ND_IT = FF // (2 * P)
    NU = NG * 8
    NB = NU // 2
    LV = 8

    w_in = w_in_d[0].rearrange("(kt p) n -> p kt n", p=P)
    w_pa = w_pa_d[0].rearrange("(kt p) n -> p kt n", p=P)
    w_pb = w_pb_d[0].rearrange("(kt p) n -> p kt n", p=P)
    w_fg = w_fg_d[0].rearrange("(kt p) n -> p kt n", p=P)
    w_fu = w_fu_d[0].rearrange("(kt p) n -> p kt n", p=P)
    w_out = w_out_d[0]
    w_fd = w_fd_d[0]
    x_t = x_d[0].rearrange("(tt p) d -> p tt d", p=P)
    out_t = out_d[0].rearrange("(tt p) d -> p tt d", p=P)

    gate_d = nc.dram_tensor("gate_scratch", (2 * NK, P, S), F32).ap()
    stat_d = nc.dram_tensor("stat_scratch", (H, 2 * NU, P), F32).ap()
    wgt_d = nc.dram_tensor("weight_scratch", (H, NG, NT, P), F32).ap()
    oa_d = nc.dram_tensor("oa_scratch", (H, P, S), F32).ap()
    ob_d = nc.dram_tensor("ob_scratch", (2 * H, P, S), F32).ap()

    ctx = ExitStack()

    def sem(name):
        return ctx.enter_context(nc.semaphore(name))

    def on(stack):
        def sb(name, shape, dt=F32):
            return stack.enter_context(nc.sbuf_tensor(name, shape, dt))
        return sb

    sb = on(ctx)
    act_hi = sb("act_hi", [P, NK, S], F32R)
    act_lo = sb("act_lo", [P, NK, S], F32R)
    w_raw = sb("w_raw", [P, 3, 1024])
    w_hi = sb("w_hi", [P, 3, 1024], F32R)
    w_lo = sb("w_lo", [P, 3, 1024], F32R)
    ident = sb("ident", [P, P])
    small = sb("small", [P, 128])
    gain1, gain2 = small[:, 0:8], small[:, 8:16]
    ssq, var, rstd = small[:, 16:24], small[:, 24:32], small[:, 32:40]
    b_a = small[:, 40:44]
    gn = small[:, 44:46]
    mhalf = small[:, 48:56]
    w_up = sb("w_up", [LR, H * P])
    ab_t = sb("ab_t", [LR, S])

    with ExitStack() as mem:
        sb = on(mem)
        cos_t = sb("cos_t", [P, NT, 64])
        sin_t = sb("sin_t", [P, NT, 64])
        q_gain = sb("q_gain", [P, P])
        k_gain = sb("k_gain", [P, P])
        near = sb("near", [P, 2 * P])
        wide = sb("wide", [P, P])
        v_raw = sb("v_raw", [P, S])
        qk_raw = sb("qk_raw", [P, 2, HALF])
        sq = sb("sq", [P, 4, P])
        qn = sb("qn", [P, 4, P])
        qg = sb("qg", [P, 4, P])
        rc = sb("rc", [P, 4, P])
        rs = sb("rs", [P, 4, P])
        rot = sb("rot", [P, 2, 4, P])
        qk_st = sb("qk_st", [P, 3, 8, 4])
        qk_t = sb("qk_t", [P, 4, S])
        vt = sb("vt", [P, NU, P])
        sm = sb("sm", [P, 2, 2, 2 * P])
        pt = sb("pt", [P, 2, 2, 2, P])
        nmax = sb("nmax", [P, NU])
        stats = sb("stats", [P, 2 * NU])
        u_t = sb("u_t", [P, NU, P])
        stat_sb = sb("stat_sb", [2 * NU, P])
        st8 = sb("st8", [NT, 2, NG, P])
        mm8 = sb("mm8", [NT, P])
        e8 = sb("e8", [NT, NG, P])
        z8 = sb("z8", [NT, NG + 1, P])
        wb = sb("wb", [P, NG, S])
        gbuf = sb("gbuf", [P, 2, HALF])
    with ExitStack() as mem:
        sb = on(mem)
        hold = sb("hold", [P, NT * 64 * 2 + 4 * P + P])
        xin = sb("xin", [P, NT, D])
        junk = sb("junk", [P, D])
        ang = sb("ang", [P, NT, 64])
        tra = sb("tra", [P, NT, 64])
        trb = sb("trb", [P, NT, 64])
        red = sb("red", [P, NT, 64])
        posi = sb("posi", [P, NT], I32)
        posf = sb("posf", [P, NT])
        invf = sb("invf", [P, 64])
        ab_raw = sb("ab_raw", [P, NK, LR])
        ab_hi = sb("ab_hi", [P, NK, LR], F32R)
        ab_lo = sb("ab_lo", [P, NK, LR], F32R)
        pari = sb("pari", [P, P], I32)
        parj = sb("parj", [P, P], I32)
        parf = sb("parf", [P, P])
    with ExitStack() as mem:
        sb = on(mem)
        gmask = sb("gmask", [P, LV, P])
        w_up_h = sb("w_up_h", [LR, P])
        b_a_h = sb("b_a_h", [P, 1])
        kf = sb("kf", [P, S])
        qf = sb("qf", [P, S])
        bcum = sb("bcum", [P, S])
        za = sb("za", [P, HALF])
        zm = sb("zm", [P, HALF])
        raw2 = sb("raw2", [P, 2, HALF])
        dbuf = sb("dbuf", [P, 8, 2 * P])
        fbuf = sb("fbuf", [P, 2, 8, 2 * P])
        qh = sb("qh", [P, S])
        elast = sb("elast", [P, 8])
        vtok = sb("vtok", [P, NT, DV])
        lvm = sb("lvm", [P, LV, P])
        att = sb("att", [P, NT, P])
        khat = sb("khat", [P, NT, P])
        state = sb("state", [P, 2, DV])
        osq = sb("osq", [P, DV])
        obn = sb("obn", [P, 2, DV])
        ost = sb("ost", [P, 3, 8])
        ob_t = sb("ob_t", [P, 2, S])
        g_t = sb("g_t", [P, 2, S])
    with ExitStack() as mem:
        sb = on(mem)
        xk = sb("xk", [P, NT, D])
        oa_hi = sb("oa_hi", [P, H, S], F32R)
        oa_lo = sb("oa_lo", [P, H, S], F32R)
        y_hi = sb("y_hi", [P, 2, S], F32R)
        y_lo = sb("y_lo", [P, 2, S], F32R)
        gl = sb("gl", [P, 2, 2, HALF])
        ya = sb("ya", [P, HALF])
        yb = sb("yb", [P, HALF])
        yf = sb("yf", [P, 2, HALF])
    with ExitStack() as mem:
        sb = on(mem)
        hold2 = sb("hold2", [P, NT, D])
        xn = sb("xn", [P, 4, D])
        junk2 = sb("junk2", [P, D])

    bank = [ctx.enter_context(nc.psum_tensor(f"bank{i}", [P, HALF], F32)) for i in range(5)]
    lvl_ps = ctx.enter_context(nc.psum_tensor("lvl_ps", [P, 2, HALF], F32))
    bank7 = ctx.enter_context(nc.psum_tensor("bank7", [P, HALF], F32))
    banks = [*(b[:, :] for b in bank), lvl_ps[:, 0, :], lvl_ps[:, 1, :], bank7[:, :]]
    s_ps, pt_ps, o_ps = banks[2], banks[3], banks[4]
    x_ps = [banks[5], banks[6]]
    ok_ps = banks[7]
    bank3 = banks[3]

    phase_end = sem("phase_end")
    raw_in = [sem(f"raw_in{i}") for i in range(3)]
    hi_done, lo_done = sem("hi_done"), sem("lo_done")
    x_in = [sem(f"x_in{i}") for i in range(4)]
    const_in = sem("const_in")
    passed = sem("passed")
    pool_const = sem("pool_const")
    par_done = sem("par_done")
    pos_step = sem("pos_step")
    sin_done = sem("sin_done")
    ssq_done, var_done, rstd_done, xn_done = sem("ssq_done"), sem("var_done"), sem("rstd_done"), sem("xn_done")
    nt_ready, nt_hi, nt_lo = sem("nt_ready"), sem("nt_hi"), sem("nt_lo")
    ab_hi_done, ab_lo_done = sem("ab_hi_done"), sem("ab_lo_done")
    ab_ready, ab_done = sem("ab_ready"), sem("ab_done")
    ab_in = sem("ab_in")
    st_ready, st_evac = sem("st_ready"), sem("st_evac")
    gate_out = [sem("gate_out0"), sem("gate_out1")]
    vtr_ready, v_evac = sem("vtr_ready"), sem("v_evac")
    t1_ready, t1_sq, t1_ss, t1_var, t1_rstd, t1_norm = (sem("t1_" + n) for n in
                                                        ("ready", "sq", "ss", "var", "rstd", "norm"))
    t1_gain, t1_cos, t1_sin, rot_done = sem("t1_gain"), sem("t1_cos"), sem("t1_sin"), sem("rot_done")
    t2_ready, t2_evac = sem("t2_ready"), sem("t2_evac")
    s_ready, masked, neg_max, p_done = sem("s_ready"), sem("masked"), sem("neg_max"), sem("p_done")
    pt_ready, pt_evac, pv_ready, u_done = sem("pt_ready"), sem("pt_evac"), sem("pv_ready"), sem("u_done")
    stat_tr, stat_sbd, stat_out, stat_in = sem("stat_tr"), sem("stat_sbd"), sem("stat_out"), sem("stat_in")
    c_step, c_diff, c_exp, c_wgt = sem("c_step"), sem("c_diff"), sem("c_exp"), sem("c_wgt")
    wgt_out, wb_in, wb_mul, wb_sum, oa_out = (sem(n) for n in ("wgt_out", "wb_in", "wb_mul", "wb_sum", "oa_out"))
    up_copied, z_ready, z_abs, z_min, z_ln, b_done = (sem(n) for n in
                                                      ("up_copied", "z_ready", "z_abs", "z_min", "z_ln", "b_done"))
    d_done, e_done, f_done, el_done = sem("d_done"), sem("e_done"), sem("f_done"), sem("el_done")
    vb_ready, vb_evac = sem("vb_ready"), sem("vb_evac")
    g_done = sem("g_done")
    l_ready, l_mask, att_done = sem("l_ready"), sem("l_mask"), sem("att_done")
    kh_ready, kh_evac = sem("kh_ready"), sem("kh_evac")
    kv_ready, state_done = sem("kv_ready"), sem("state_done")
    o_sq, o_var, o_rstd, obn_done = sem("o_sq"), sem("o_var"), sem("o_rstd"), sem("obn_done")
    obt_ready, obt_evac, ob_gated, ob_out = sem("obt_ready"), sem("obt_evac"), sem("ob_gated"), sem("ob_out")
    stage_in = [sem(f"stage_in{i}") for i in range(8)]
    stage_hi, stage_lo = sem("stage_hi"), sem("stage_lo")
    xk_in = sem("xk_in")
    gl_in = [sem("gl_in0"), sem("gl_in1")]
    sig_done = sem("sig_done")
    mix_ready, mix_step, y_done, yhi_done, ylo_done = (sem(n) for n in
                                                       ("mix_ready", "mix_step", "y_done", "yhi_done", "ylo_done"))
    down_ready, acc_done = sem("down_ready"), sem("acc_done")
    out_done = sem("out_done")

    block = ctx.enter_context(nc.Block())

    def enter_phase(eng, k):
        eng.wait_ge(phase_end, 4 * k)

    def alone(eng):
        eng.sem_inc(passed, 1)

    def leave_phase(eng):
        eng.drain().then_inc(phase_end, 1)

    JOBS_A = {2: ["v0", "v1"], 3: ["v2", "a0"], 4: ["v3", "a1"], 5: ["v4", "a2", "b0"],
              6: ["v5", "a3", "b1"], 7: ["a4", "b2"], 8: ["a5", "b3", "s0"], 9: ["a6", "b4", "s1"],
              10: ["a7", "b5", "s2"], 11: ["b6", "s3", "s4"], 12: ["b7", "s5"], 13: ["s6"],
              14: ["s7", "s8"], 15: ["s9"], 16: ["s10", "s11"], 17: ["s12", "s13"]}
    X_ORDER = [j for s in sorted(JOBS_A) for j in JOBS_A[s] if j[0] in "vab"]
    JOBS_B = {0: ["z0"], 1: ["z1"], 4: ["l0"], 5: ["v0", "l1"], 6: ["v1", "l2"], 7: ["v2", "l3"],
              8: ["v3", "m0", "l4"], 9: ["t0", "m1", "l5"], 10: ["t1", "m2", "l6"], 11: ["t2", "m3", "l7"]}
    TAIL_B = {0: ["t3", "m4"], 1: ["t4", "m5"], 2: ["t5", "m6"], 3: ["t6", "m7"], 4: ["t7"]}

    def jobs_b(s, h, tail):
        own = [(j[0], int(j[1:]), h) for j in JOBS_B.get(s, [])]
        old = [(j[0], int(j[1:]), h - 1) for j in TAIL_B.get(s, [])] if tail else []
        return old + own if s == 4 else own + old

    def rest_b():
        return [(j[0], int(j[1:])) for s in range(5) for j in TAIL_B[s]]

    def slot_of(k):
        return k % 3

    def unit(b, i):
        u = 2 * b + i
        g, n = u // 8, u % 8
        return g, n, (g == 0 and n > 0) or (g == 1 and n % 2 == 1)

    def tokens(t, g, n):
        if g == 0:
            return t[:, P * n:P * n + P]
        if g == 1:
            r, b = n // 2, n % 2
            return t[:, 4 * P * b + r:4 * P * b + r + 4 * P - 3:4]
        return t[:, n:n + 8 * P - 7:8]

    @block.sync
    def _(sp):
        for i in range(4):
            sp.dma_start(xin[:, 2 * i:2 * i + 2, :], x_t[:, 2 * i:2 * i + 2, :]).then_inc(x_in[i], 16)
        sp.dma_start(ab_raw[:, :, :], w_in[:, :, C_AB:C_AB + LR]).then_inc(ab_in, 16)

        def load(n, k, src, parts=None):
            dst = w_raw[:, slot_of(k), :] if parts is None else w_raw[:, slot_of(k), 0:parts]
            if len(src.shape) == 3:
                dst = dst.rearrange("p (kt n) -> p kt n", n=P)
            sp.dma_start(dst, src).then_inc(raw_in[slot_of(k)], 16)

        def free(n):
            sp.wait_ge(lo_done, n - 2)
            alone(sp)

        def load_a(h, k):
            cols = [C_V + P * h, C_K + P * h, P * h, W_KV + P * h, 2 * W_KV + P * h,
                    C_G + 4 * P * h, C_G + 4 * P * h + P, C_G + 4 * P * h + 2 * P, C_G + 4 * P * h + 3 * P]
            load(A0 + TA * h + k, k, w_in[:, :, bass.ds(cols[k], P)])

        for k in range(3):
            load_a(0, k)
        for k in range(3, TA):
            free(k)
            load_a(0, k)
        with sp.Fori(1, H) as h:
            for k in range(TA):
                free(A0 + TA * h + k)
                load_a(h, k)
        with sp.Fori(0, H) as h:
            cols = [C_KB + P * h, C_QB + P * h, C_VB + DV * h, C_VB + DV * h + P,
                    C_RB + DV * h, C_RB + DV * h + P]
            for k in range(TB):
                free(B0 + TB * h + k)
                load(B0 + TB * h + k, k, w_in[:, :, bass.ds(cols[k], P)])
        with sp.Fori(0, NC_IT) as i:
            for k in range(TC):
                free(C0 + TC * i + k)
                f = k // 2
                if k in (0, 2):
                    load(0, k, w_pa[:, :, bass.ds(2 * P * i + P * f, P)], parts=H * P)
                elif k in (1, 3):
                    load(0, k, w_pb[:, :, bass.ds(2 * P * i + P * f, P)])
                else:
                    load(0, k, w_out[bass.ds(2 * P * i + P * (k - 4), P), :])
        with sp.Fori(0, ND_IT) as i:
            for k in range(TC):
                free(D0 + TC * i + k)
                f = k // 2
                if k in (0, 2):
                    load(0, k, w_fg[:, :, bass.ds(2 * P * i + P * f, P)])
                elif k in (1, 3):
                    load(0, k, w_fu[:, :, bass.ds(2 * P * i + P * f, P)])
                else:
                    load(0, k, w_fd[bass.ds(2 * P * i + P * (k - 4), P), :])
        for tt in range(NT):
            sp.wait_ge(acc_done, 16 * (NC_IT + ND_IT - 1) + 2 * tt + 2)
            sp.dma_start(out_t[:, tt, :], xk[:, tt, :]).then_inc(out_done, 16)
        sp.wait_ge(out_done, 16 * NT)

    @block.gpsimd
    def _(pool):
        pool.dma_start(posi[:, :], pos_d[0].rearrange("(tt p) -> p tt", p=P),
                       allow_slow_non_contiguous=True).then_inc(const_in, 16)
        pool.dma_start(invf[:, :], inv_freq_d[:].partition_broadcast(P)).then_inc(const_in, 16)
        pool.dma_start(gain1, norm1_d[0].rearrange("(kt p) -> p kt", p=P),
                       allow_slow_non_contiguous=True).then_inc(const_in, 16)
        pool.dma_start(gain2, norm2_d[0].rearrange("(kt p) -> p kt", p=P),
                       allow_slow_non_contiguous=True).then_inc(const_in, 16)
        pool.dma_start(b_a, b_a_d[0].rearrange("(h p) -> p h", p=P),
                       allow_slow_non_contiguous=True).then_inc(const_in, 16)
        pool.dma_start(gn, gn_d[0].rearrange("(e p) -> p e", p=P),
                       allow_slow_non_contiguous=True).then_inc(const_in, 16)
        pool.dma_start(q_gain[:, :], qn_d[0].partition_broadcast(P)).then_inc(const_in, 16)
        pool.dma_start(k_gain[:, :], kn_d[0].partition_broadcast(P)).then_inc(const_in, 16)
        pool.dma_start(w_up[:, :], w_up_d[0]).then_inc(const_in, 16)
        pool.memset(ident[:, :], 0.0).then_inc(pool_const, 1)
        pool.memset(mhalf, -0.5).then_inc(pool_const, 1)
        pool.memset(near[:, :], 0.0).then_inc(pool_const, 1)
        pool.iota(pari[:, :], pattern=[[1, P]], base=P, channel_multiplier=-1).then_inc(pool_const, 1)
        pool.wait_ge(pool_const, 4)
        pool.affine_select(out=ident[:, :], in_=ident[:, :], compare_op=ALU.not_equal, fill=1.0, base=0,
                           pattern=[[-1, P]], channel_multiplier=1).then_inc(pool_const, 1)
        pool.affine_select(out=near[:, :], in_=near[:, :], compare_op=ALU.is_ge, fill=NEG, base=0,
                           pattern=[[1, 2 * P]], channel_multiplier=-1).then_inc(pool_const, 1)
        pool.wait_ge(pool_const, 6)
        pool.affine_select(out=near[:, :], in_=near[:, :], compare_op=ALU.is_ge, fill=NEG, base=P,
                           pattern=[[-1, 2 * P]], channel_multiplier=1).then_inc(pool_const, 1)
        pool.wait_ge(par_done, 2)
        pool.affine_select(out=wide[:, :], in_=parf[:, :], compare_op=ALU.is_ge, fill=NEG, base=0,
                           pattern=[[-1, P]], channel_multiplier=1).then_inc(pool_const, 1)
        for i in range(4):
            pool.wait_ge(var_done, i + 1)
            pool.tensor_tensor(rstd[:, 2 * i:2 * i + 2], var[:, 2 * i:2 * i + 2], mhalf[:, 0:2],
                               ALU.pow).then_inc(rstd_done, 1)
        leave_phase(pool)
        enter_phase(pool, 1)

        with pool.Fori(0, H) as h:
            for j in range(8):
                n = 8 * h + j
                pool.wait_ge(t1_var, n + 1)
                pool.tensor_tensor(qk_st[:, 2, j, :], qk_st[:, 1, j, :], mhalf[:, 0:4],
                                   ALU.pow).then_inc(t1_rstd, 1)
                pool.wait_ge(t1_norm, n + 1)
                pool.wait_ge(t1_cos, n)
                pool.wait_ge(t1_sin, 2 * n)
                gain = k_gain if j < 2 else q_gain
                pool.tensor_tensor(qg[:, :, :], qn[:, :, :], gain[:, None, :].broadcast_to([P, 4, P]),
                                   ALU.mult).then_inc(t1_gain, 1)
                pool.wait_ge(t1_gain, n + 1)
                pool.wait_ge(rot_done, 2 * n)
                sin_b = sin_t[:, 4 * (j % 2):4 * (j % 2) + 4, :]
                pool.tensor_tensor(rs[:, :, 0:64], qg[:, :, 64:128], sin_b, ALU.mult).then_inc(t1_sin, 1)
                pool.tensor_tensor(rs[:, :, 64:128], qg[:, :, 0:64], sin_b, ALU.mult).then_inc(t1_sin, 1)
            sd = stat_d[bass.ds(h, 1)].rearrange("a u q -> (a u) q")
            pool.wait_ge(stat_sbd, h + 1)
            alone(pool)
            pool.dma_start(sd, stat_sb[:, :]).then_inc(stat_out, 16)
            pool.wait_ge(stat_out, 16 * h + 16)
            pool.wait_ge(c_wgt, 3 * h)
            alone(pool)
            for q in range(2):
                r0 = NU * q
                pool.dma_start(st8[:, q, 0, :], sd[r0:r0 + 8, :]).then_inc(stat_in, 16)
                for b in range(2):
                    pool.dma_start(st8[4 * b:4 * b + 4, q, 1, :].rearrange("c (r jl) -> c r jl", jl=32),
                                   sd[r0 + 8 + b:r0 + 16:2, :].rearrange("r (jh jl) -> jh r jl", jl=32)
                                   ).then_inc(stat_in, 16)
                pool.dma_start(st8[:, q, 2, :].rearrange("c (r il) -> c r il", il=16),
                               sd[r0 + 16:r0 + 24, :].rearrange("r (ih il) -> ih r il", il=16)
                               ).then_inc(stat_in, 16)
            pool.wait_ge(c_wgt, 3 * h + 3)
            alone(pool)
            wd = wgt_d[bass.ds(h, 1)].rearrange("a g c t -> (a g) c t")
            pool.dma_start(wd.rearrange("g c t -> c g t"), e8[:, :, :]).then_inc(wgt_out, 16)
            pool.wait_ge(wgt_out, 16 * h + 16)
            pool.wait_ge(oa_out, 16 * h)
            alone(pool)
            pool.dma_start(wb[:, :, :], wd.rearrange("g c t -> g (c t)").partition_broadcast(P)
                           ).then_inc(wb_in, 16)
            pool.wait_ge(wb_mul, 3 * h + 3)
            pool.tensor_tensor(wb[:, 0, :], wb[:, 0, :], wb[:, 1, :], ALU.add).then_inc(wb_sum, 1)
            pool.wait_ge(wb_sum, 2 * h + 1)
            pool.tensor_tensor(wb[:, 0, :], wb[:, 0, :], wb[:, 2, :], ALU.add).then_inc(wb_sum, 1)
            pool.wait_ge(wb_sum, 2 * h + 2)
            alone(pool)
            pool.dma_start(oa_d[bass.ds(h, 1)].rearrange("a p t -> (a p) t"), wb[:, 0, :]).then_inc(oa_out, 16)
        pool.wait_ge(oa_out, 16 * H)
        leave_phase(pool)
        enter_phase(pool, 2)

        nm0 = 8
        pool.memset(gmask[:, 0:7, :], 1.0).then_inc(pool_const, 1)
        pool.memset(gmask[:, 7, :], 0.0).then_inc(pool_const, 1)
        pool.wait_ge(pool_const, nm0 + 2)
        for lv in range(7):
            m = 64 >> lv
            v = gmask[:, lv, :].rearrange("p (n two m) -> p n two m", two=2, m=m)
            nblk = P // (2 * m)
            pool.memset(v[:, :, 0, :], 0.0).then_inc(pool_const, 1)
            pool.affine_select(out=v[:, :, 1, :], in_=v[:, :, 1, :], compare_op=ALU.is_ge, fill=0.0, base=0,
                               pattern=[[-2 * m, nblk], [0, m]], channel_multiplier=1).then_inc(pool_const, 1)
        pool.affine_select(out=gmask[:, 7, :], in_=gmask[:, 7, :], compare_op=ALU.not_equal, fill=1.0, base=0,
                           pattern=[[-1, P]], channel_multiplier=1).then_inc(pool_const, 1)
        pool.wait_ge(pool_const, nm0 + 17)
        for lv in range(7):
            m = 64 >> lv
            v = gmask[:, lv, :].rearrange("p (n two m) -> p n two m", two=2, m=m)
            pool.affine_select(out=v[:, :, 1, :], in_=v[:, :, 1, :], compare_op=ALU.is_ge, fill=0.0, base=m - 1,
                               pattern=[[2 * m, P // (2 * m)], [0, m]], channel_multiplier=-1
                               ).then_inc(pool_const, 1)
        def pool_head(h, tail):
            def pool_d(p):
                for lv in range(8):
                    n = 32 * h + 8 * p + lv
                    m = 64 >> lv if lv < 7 else 64
                    if p == 0:
                        pool.wait_ge(f_done, 36 * h)
                        if lv == 0:
                            pool.wait_ge(b_done, 8 * h + 8)
                    else:
                        pool.wait_ge(f_done, 36 * h + 9 * (p - 1) + lv + 1)
                    bp = bcum[:, 2 * P * p:2 * P * p + 2 * P]
                    dst = dbuf[:, lv, :]
                    if lv < 7:
                        bv = bp.rearrange("p (n two m) -> p n two m", two=2, m=m)
                        dv = dst.rearrange("p (n two m) -> p n two m", two=2, m=m)
                        ref = bv[:, :, 0, m - 1:m].broadcast_to([P, P // m, m])
                        pool.tensor_tensor(dv[:, :, 0, :], ref, bv[:, :, 0, :], ALU.subtract).then_inc(d_done, 1)
                        pool.tensor_tensor(dv[:, :, 1, :], bv[:, :, 1, :], ref, ALU.subtract).then_inc(d_done, 1)
                    else:
                        bv = bp.rearrange("p (n m) -> p n m", m=P)
                        dv = dst.rearrange("p (n m) -> p n m", m=P)
                        ref = bv[:, :, P - 1:P].broadcast_to([P, 2, P])
                        pool.tensor_tensor(dv, ref, bv, ALU.subtract).then_inc(d_done, 2)

            work = ["d0", "d1", "d2", "d3", "o0", "o1", "o2", "o3"]
            if tail:
                work = ["O4", "O5", "d0", "O6", "d1", "O7", "d2", "G0", "d3"] + work[4:]
            for w in work:
                if w[0] == "d":
                    pool_d(int(w[1]))
                elif w[0] == "o":
                    pool_o(h, int(w[1]))
                elif w[0] == "O":
                    pool_o(h - 1, int(w[1]))
                else:
                    pool_out(h - 1)

        def pool_o(h, c):
            pool.wait_ge(o_var, 8 * h + c + 1)
            pool.tensor_tensor(ost[:, 2, c:c + 1], ost[:, 1, c:c + 1], mhalf[:, 0:1],
                               ALU.pow).then_inc(o_rstd, 1)

        def pool_out(h):
            pool.wait_ge(ob_gated, 4 * h + 4)
            alone(pool)
            pool.dma_start(ob_d[bass.ds(2 * h, 2)].rearrange("e p t -> p e t"), ob_t[:, :, :]
                           ).then_inc(ob_out, 16)

        pool_head(0, False)
        with pool.Fori(1, H) as h:
            pool_head(h, True)
        for c in range(4, 8):
            pool_o(H - 1, c)
        pool_out(H - 1)
        pool.wait_ge(ob_out, 16 * H)
        leave_phase(pool)
        enter_phase(pool, 3)

        for i in range(12):
            if i >= 8:
                pool.wait_ge(stage_lo, i - 7)
            src = oa_d[i] if i < H else ob_d[i - H]
            pool.dma_start(xk[:, i % 8, :], src).then_inc(stage_in[i % 8], 16)
        pool.wait_ge(stage_lo, 12)
        pool.dma_start(xk[:, :, :], x_t).then_inc(xk_in, 16)
        gd = gate_d.rearrange("(ab f) p t -> f p ab t", ab=2)
        with pool.Fori(0, NC_IT) as i:
            for w in range(4):
                f, xh = w // 2, w % 2
                pool.wait_ge(y_done, 4 * i if w < 2 else 4 * i + w - 1)
                alone(pool)
                src = gd[bass.ds(2 * i + f, 1)].rearrange("a p ab t -> (a p) ab t")
                pool.dma_start(gl[:, xh, :, :], src[:, :, HALF * xh:HALF * xh + HALF]).then_inc(gl_in[xh], 16)
        leave_phase(pool)
        enter_phase(pool, 4)
        for i in range(4):
            pool.wait_ge(var_done, 4 + i + 1)
            pool.tensor_tensor(rstd[:, 2 * i:2 * i + 2], var[:, 2 * i:2 * i + 2], mhalf[:, 0:2],
                               ALU.pow).then_inc(rstd_done, 1)
        leave_phase(pool)

    @block.scalar
    def _(act):
        def hi_tile(k, turn, width=1024):
            act.wait_ge(raw_in[slot_of(k)], 16 * turn)
            act.copy(w_hi[:, slot_of(k), 0:width], w_raw[:, slot_of(k), 0:width]).then_inc(hi_done, 1)

        def norm_hi(j, xt, gain, jk):
            for tt in range(NT):
                n = 8 * j + tt
                if j == 0 and tt % 2 == 0:
                    act.wait_ge(x_in[tt // 2], 16)
                if n % 8:
                    act.wait_ge(ssq_done, n)
                act.activation(jk[:, :], xt[:, tt, :], ACT.Square,
                               accum_out=ssq[:, tt:tt + 1]).then_inc(ssq_done, 1)
            for g in range(2 * NK):
                xh, kt = g // NK, g % NK
                act.wait_ge(nt_ready, 16 * j + g + 1)
                act.activation(act_hi[:, kt, HALF * xh:HALF * xh + HALF], banks[g % 8], ACT.Copy,
                               scale=gain[:, kt:kt + 1]).then_inc(nt_hi, 1)

        act.wait_ge(pos_step, 9)
        act.activation(sin_t[:, :, :], tra[:, :, :], ACT.Sin).then_inc(sin_done, 1)
        act.wait_ge(pos_step, 16)
        act.activation(cos_t[:, :, :], trb[:, :, :], ACT.Sin).then_inc(sin_done, 1)
        act.preload_act_table_set("natural_log_exp_and_others")
        act.wait_ge(const_in, 16 * 9)
        norm_hi(0, xin, gain1, junk)
        act.wait_ge(ab_in, 16)
        act.copy(ab_hi[:, :, :], ab_raw[:, :, :]).then_inc(ab_hi_done, 1)
        hi_tile(0, 1)
        hi_tile(1, 1)
        act.wait_ge(ab_ready, 2)
        act.copy(ab_t[:, 0:HALF], banks[0][0:LR, :]).then_inc(ab_done, 1)
        act.copy(ab_t[:, HALF:S], banks[1][0:LR, :]).then_inc(ab_done, 1)
        leave_phase(act)
        enter_phase(act, 1)

        with act.Fori(0, H) as h:
            for s in range(2 * TA):
                k, xh = s // 2, s % 2
                if xh == 0:
                    act.wait_ge(st_ready, 2 * TA * h + 2 * k)
                    hi_tile(k + 2, 3 * h + (k + 2) // 3 + 1)
                act.wait_ge(st_ready, 2 * TA * h + s + 1)
                if k == 0:
                    act.wait_ge(vtr_ready, 6 * h)
                    dst = v_raw[:, HALF * xh:HALF * xh + HALF]
                elif k <= 4:
                    j = s - 2
                    act.wait_ge(t1_ready, 8 * h + (j - 1 if j >= 2 else 0))
                    dst = qk_raw[:, xh, :]
                else:
                    act.wait_ge(gate_out[xh], 16 * (4 * h + k - 5))
                    dst = gbuf[:, xh, :]
                act.copy(dst, banks[xh]).then_inc(st_evac, 1)
                if k > 4:
                    act.wait_ge(st_evac, 2 * TA * h + s + 1)
                    act.dma_start(gate_d[bass.ds(4 * h + k - 5, 1)].rearrange("a p t -> (a p) t")
                                  [:, HALF * xh:HALF * xh + HALF], gbuf[:, xh, :]).then_inc(gate_out[xh], 16)
                for job in JOBS_A.get(s, []):
                    j = int(job[1:])
                    if job[0] == "v":
                        act.wait_ge(vtr_ready, 6 * h + j + 1)
                        act.wait_ge(pv_ready, NB * h)
                        act.copy(vt[:, 4 * j:4 * j + 4, :],
                                 x_ps[X_ORDER.index(job) % 2].rearrange("p (u d) -> p u d", d=P)
                                 ).then_inc(v_evac, 1)
                    elif job[0] == "a":
                        act.wait_ge(t1_ready, 8 * h + j + 1)
                        act.wait_ge(t1_ss, 8 * h + j)
                        act.activation(sq[:, :, :],
                                       x_ps[X_ORDER.index(job) % 2].rearrange("p (t d) -> p t d", d=P),
                                       ACT.Square).then_inc(t1_sq, 1)
                    elif job[0] == "b":
                        act.wait_ge(t2_ready, 8 * h + j + 1)
                        act.wait_ge(s_ready, NB * h)
                        act.copy(qk_t[:, j // 2, HALF * (j % 2):HALF * (j % 2) + HALF],
                                 x_ps[X_ORDER.index(job) % 2]).then_inc(t2_evac, 1)
                    else:
                        if 1 <= j <= NB:
                            b = j - 1
                            act.wait_ge(pt_ready, NB * h + b + 1)
                            act.wait_ge(pv_ready, NB * h + (b - 1 if b >= 2 else 0))
                            if b >= 8:
                                o, i_ = pt[:, b % 2, :, 1, :], pt_ps.rearrange(
                                    "p (i k q) -> p i k q", i=2, k=2)[:, :, 1, :]
                            else:
                                lo = P if (b == 0 or b >= 4) else 0
                                o = pt[:, b % 2, :, :, :].rearrange("p i k q -> p (i k q)")[:, lo:]
                                i_ = pt_ps[:, lo:]
                            act.copy(o, i_).then_inc(pt_evac, 1)
                        if j < NB:
                            act.wait_ge(neg_max, NB * h + j + 1)
                            for i in range(2):
                                g, _, prev = unit(j, i)
                                lo = 0 if prev else P
                                u = 2 * j + i
                                t = sm[:, j % 2, i, lo:]
                                act.activation(t, t, ACT.Exp, bias=nmax[:, u:u + 1], scale=SCALE,
                                               accum_out=stats[:, NU + u:NU + u + 1]).then_inc(p_done, 1)
            act.wait_ge(stat_tr, h + 1)
            act.wait_ge(stat_out, 16 * h)
            act.copy(stat_sb[:, :], pt_ps[0:2 * NU, 0:P]).then_inc(stat_sbd, 1)
            for g in range(NG):
                act.wait_ge(c_diff, 3 * h + g + 1)
                act.activation(e8[:, g, :], e8[:, g, :], ACT.Exp, scale=SCALE).then_inc(c_exp, 1)
        act.wait_ge(gate_out[0], 16 * 2 * NK)
        act.wait_ge(gate_out[1], 16 * 2 * NK)
        leave_phase(act)
        enter_phase(act, 2)

        def act_head(h, tail):
            base = 2 * B0 + 2 * TB * h
            act.wait_ge(z_ready, 2 * h)
            act.wait_ge(z_min, 2 * h)
            act.copy(w_up_h[:, :], w_up[:, bass.ds(P * h, P)]).then_inc(up_copied, 1)
            act.copy(b_a_h[:, :], b_a[:, bass.ds(h, 1)]).then_inc(up_copied, 1)

            def act_z(xh):
                n = 2 * h + xh
                act.wait_ge(z_ready, n + 1)
                act.wait_ge(b_done, 8 * h + 4 * xh)
                act.wait_ge(up_copied, 2 * h + 2)
                act.activation(za[:, :], o_ps, ACT.Abs, bias=b_a_h[:, 0:1]).then_inc(z_abs, 1)
                act.wait_ge(z_abs, n + 1)
                act.activation(za[:, :], za[:, :], ACT.Exp, scale=-1.0).then_inc(z_ln, 1)
                act.wait_ge(z_ln, 2 * n + 1)
                act.activation(za[:, :], za[:, :], ACT.Ln, bias=1.0).then_inc(z_ln, 1)

            def act_e(p):
                for lv in range(8):
                    act.wait_ge(d_done, 64 * h + 16 * p + 2 * lv + 2)
                    t = dbuf[:, lv, :]
                    act.activation(t, t, ACT.Exp, scale=1.0 / TEMP).then_inc(e_done, 1)
                t = qh[:, 2 * P * p:2 * P * p + 2 * P]
                if tail:
                    act.wait_ge(kv_ready, 8 * (h - 1) + 2 * p + 2)
                act.activation(t, bcum[:, 2 * P * p:2 * P * p + 2 * P], ACT.Exp,
                               scale=1.0 / TEMP).then_inc(e_done, 1)
                if tail:
                    act.wait_ge(state_done, 8 * (h - 1) + 2 * p + 2)
                act.activation(elast[:, 2 * p:2 * p + 2], bcum[:, 2 * P * p + P - 1:2 * P * p + 2 * P:P],
                               ACT.Exp, scale=1.0 / TEMP).then_inc(el_done, 1)

            for s in range(2 * TB):
                k, xh = s // 2, s % 2
                if xh == 0:
                    act.wait_ge(st_ready, base + 2 * k)
                    hi_tile(k + 2, B0 // 3 + 2 * h + (k + 2) // 3 + 1)
                act.wait_ge(st_ready, base + s + 1)
                if k == 0:
                    act.wait_ge(l_ready, 8 * h)
                    act.copy(kf[:, HALF * xh:HALF * xh + HALF], banks[xh]).then_inc(st_evac, 1)
                elif k == 1:
                    act.mul(qf[:, HALF * xh:HALF * xh + HALF], banks[xh], SCALE).then_inc(st_evac, 1)
                else:
                    if s < 8:
                        act.wait_ge(vb_ready, 4 * h + (s - 5 if s >= 6 else 0))
                        act.copy(raw2[:, xh, :], banks[xh]).then_inc(st_evac, 1)
                    else:
                        act.wait_ge(ob_gated, 4 * h)
                        act.copy(g_t[:, (s - 8) // 2, HALF * xh:HALF * xh + HALF], banks[xh]).then_inc(st_evac, 1)
                for kind, j, jh in jobs_b(s, h, tail):
                    if kind == "z":
                        act_z(j)
                    elif kind == "v":
                        e, vh = j // 2, j % 2
                        act.wait_ge(vb_ready, 4 * h + j + 1)
                        act.wait_ge(kv_ready, 8 * h)
                        act.copy(vtok[:, 4 * vh:4 * vh + 4, P * e:P * e + P],
                                 bank3.rearrange("p (c d) -> p c d", d=P)).then_inc(vb_evac, 1)
                    elif kind == "l":
                        act.wait_ge(kh_ready, 8 * h + j + 1)
                        act.wait_ge(kv_ready, 8 * h)
                        act.copy(khat[:, j, :], s_ps[:, P * (j % 4):P * (j % 4) + P]).then_inc(kh_evac, 1)
                    else:
                        (act_m if kind == "m" else act_t)(jh, j)
                if s in E_AFTER:
                    act_e(E_AFTER[s])
                if tail and s == 2:
                    act_silu(h - 1)

        E_AFTER = {2: 0, 3: 1, 5: 2, 6: 3}

        def act_silu(h):
            act.wait_ge(st_evac, 2 * B0 + 2 * TB * (h + 1))
            act.activation(g_t[:, :, :], g_t[:, :, :], ACT.Silu).then_inc(g_done, 1)
            act.preload_act_table_set("natural_log_exp_and_others")

        def act_m(h, j):
            n = 8 * h + j
            act.wait_ge(kv_ready, n + 1)
            act.wait_ge(o_sq, n)
            act.activation(osq[:, :], ok_ps[:, 0:DV], ACT.Square,
                           accum_out=ost[:, 0, j:j + 1]).then_inc(o_sq, 1)
            act.wait_ge(o_rstd, n + 1)
            act.wait_ge(obt_ready, 8 * h + (j - 1 if j >= 2 else 0))
            act.activation(obn[:, j % 2, :], ok_ps[:, 0:DV], ACT.Copy,
                           scale=ost[:, 2, j:j + 1]).then_inc(obn_done, 1)

        def act_t(h, j):
            act.wait_ge(obt_ready, 8 * h + j + 1)
            act.wait_ge(ob_out, 16 * h)
            act.copy(ob_t[:, :, P * j:P * j + P],
                     bank3[:, 0:2 * P].rearrange("p (e t) -> p e t", e=2)).then_inc(obt_evac, 1)

        act_head(0, False)
        with act.Fori(1, H) as h:
            act_head(h, True)
        for kind, j in rest_b():
            (act_m if kind == "m" else act_t)(H - 1, j)
            if kind == "t" and j == 6:
                act_silu(H - 1)
        leave_phase(act)
        enter_phase(act, 3)

        for i in range(12):
            act.wait_ge(stage_in[i % 8], 16 * (i // 8 + 1))
            dst = oa_hi[:, i, :] if i < H else act_hi[:, i - H, :]
            act.copy(dst, xk[:, i % 8, :]).then_inc(stage_hi, 1)

        def pair_loop(i, it0, first, turn0, last, fn):
            for k in range(TC):
                if k == 0:
                    act.wait_ge(down_ready, 16 * (it0 + i))
                elif k < 5:
                    act.wait_ge(mix_ready, 8 * (it0 + i) + 2 * k)
                else:
                    act.wait_ge(down_ready, 16 * (it0 + i) + 16)
                if not (last and k >= 4):
                    hi_tile(k + 2, turn0 + 2 * i + (k + 2) // 3 + 1)
                fn(k)

        def hi_y(it, w):
            f, xh = w // 2, w % 2
            act.wait_ge(y_done, 4 * it + w + 1)
            act.wait_ge(down_ready, 16 * it)
            act.copy(y_hi[:, f, HALF * xh:HALF * xh + HALF], yf[:, xh, :]).then_inc(yhi_done, 1)

        with act.Fori(0, NC_IT) as i:
            def merge(k):
                if k in (0, 2):
                    for xh in range(2):
                        act.wait_ge(gl_in[xh], 16 * (2 * i + k // 2 + 1))
                        act.activation(gl[:, xh, :, :], gl[:, xh, :, :], ACT.Sigmoid).then_inc(sig_done, 1)
                if k in (1, 3):
                    hi_y(i, k - 1)
                    hi_y(i, k)
            pair_loop(i, 0, C0, C0 // 3, False, merge)
        leave_phase(act)
        enter_phase(act, 4)
        act.wait_ge(acc_done, 16 * NC_IT)
        norm_hi(1, xk, gain2, junk2)
        leave_phase(act)
        enter_phase(act, 5)

        def ffn(i, last):
            it = NC_IT + i

            def silu(k):
                if k in (0, 2):
                    for xh in range(2):
                        w = k + xh
                        act.wait_ge(mix_ready, 8 * it + 4 * (k // 2) + xh + 1)
                        act.wait_ge(y_done, 4 * it + (w - 1 if w >= 2 else 0))
                        act.activation(gl[:, xh, 0, :], banks[xh], ACT.Silu).then_inc(sig_done, 1)
                if k in (1, 3):
                    hi_y(it, k - 1)
                    hi_y(it, k)
            pair_loop(i, NC_IT, D0, D0 // 3, last, silu)

        with act.Fori(0, ND_IT - 1) as i:
            ffn(i, False)
        ffn(ND_IT - 1, True)

    @block.vector
    def _(dve):
        def lo_tile(n, k, width=1024):
            dve.wait_ge(hi_done, n + 1)
            dve.tensor_tensor(w_lo[:, slot_of(k), 0:width], w_raw[:, slot_of(k), 0:width],
                              w_hi[:, slot_of(k), 0:width].bitcast(F32), ALU.subtract).then_inc(lo_done, 1)

        def norm_lo(j, xt, xo, gain):
            for i in range(4):
                dve.wait_ge(ssq_done, 8 * j + 2 * i + 2)
                dve.tensor_scalar(var[:, 2 * i:2 * i + 2], ssq[:, 2 * i:2 * i + 2], 1.0 / D, EPS,
                                  ALU.mult, ALU.add).then_inc(var_done, 1)
            for xh in range(2):
                if xh and j:
                    dve.wait_ge(nt_ready, 16 * j + NK)
                for tt in range(4 * xh, 4 * xh + 4):
                    if tt % 2 == 0:
                        dve.wait_ge(rstd_done, 4 * j + tt // 2 + 1)
                    dve.tensor_scalar(xo[:, tt % xo.shape[1], :], xt[:, tt, :], rstd[:, tt:tt + 1], None,
                                      ALU.mult).then_inc(xn_done, 1)
                for kt in range(NK):
                    g = NK * xh + kt
                    dve.wait_ge(nt_hi, 16 * j + g + 1)
                    hs = act_hi[:, kt, HALF * xh:HALF * xh + HALF].bitcast(F32)
                    dve.scalar_tensor_tensor(out=act_lo[:, kt, HALF * xh:HALF * xh + HALF], in0=banks[g % 8],
                                             scalar=gain[:, kt:kt + 1], in1=hs, op0=ALU.mult,
                                             op1=ALU.subtract).then_inc(nt_lo, 1)

        dve.wait_ge(const_in, 16 * 9)
        steps = [0]

        def step(ins):
            steps[0] += 1
            ins.then_inc(pos_step, 1)
            dve.wait_ge(pos_step, steps[0])

        step(dve.tensor_copy(posf[:, :], posi[:, :]))
        step(dve.tensor_tensor(ang[:, :, :], posf[:, :, None].broadcast_to([P, NT, 64]),
                               invf[:, None, :].broadcast_to([P, NT, 64]), ALU.mult))
        for shift, t in ((0.0, tra), (0.25, trb)):
            tt_ = t[:, :, :]
            step(dve.tensor_scalar(tt_, ang[:, :, :], 1.0 / TWO_PI, shift, ALU.mult, ALU.add))
            step(dve.tensor_scalar(tt_, tt_, ROUND, -ROUND, ALU.add, ALU.add))
            r1 = red[:, :, :]
            step(dve.scalar_tensor_tensor(out=r1, in0=tt_, scalar=-PI_C1, in1=ang[:, :, :],
                                          op0=ALU.mult, op1=ALU.add))
            step(dve.scalar_tensor_tensor(out=r1, in0=tt_, scalar=-PI_C2, in1=r1, op0=ALU.mult, op1=ALU.add))
            step(dve.scalar_tensor_tensor(out=r1, in0=tt_, scalar=-PI_C3, in1=r1, op0=ALU.mult, op1=ALU.add))
            step(dve.tensor_scalar(tt_, r1, shift * TWO_PI, PI_SAFE, ALU.add, ALU.min))
            step(dve.tensor_scalar(tt_, tt_, -PI_SAFE, None, ALU.max))
        dve.wait_ge(pool_const, 4)
        dve.tensor_scalar(parj[:, :], pari[:, :], 1, None, ALU.bitwise_and).then_inc(par_done, 1)
        dve.wait_ge(par_done, 1)
        dve.tensor_scalar(parf[:, :], parj[:, :], NEG, None, ALU.mult).then_inc(par_done, 1)
        norm_lo(0, xin, xin, gain1)
        dve.wait_ge(ab_hi_done, 1)
        dve.tensor_tensor(ab_lo[:, :, :], ab_raw[:, :, :], ab_hi[:, :, :].bitcast(F32),
                          ALU.subtract).then_inc(ab_lo_done, 1)
        lo_tile(0, 0)
        lo_tile(1, 1)
        leave_phase(dve)
        enter_phase(dve, 1)

        with dve.Fori(0, H) as h:
            for s in range(2 * TA):
                k, xh = s // 2, s % 2
                if xh == 0:
                    lo_tile(TA * h + k + 2, k + 2)
                for job in JOBS_A.get(s, []):
                    j = int(job[1:])
                    if job[0] == "a":
                        n = 8 * h + j
                        ps = x_ps[X_ORDER.index(job) % 2].rearrange("p (t d) -> p t d", d=P)
                        dve.wait_ge(t1_sq, n + 1)
                        dve.tensor_reduce(qk_st[:, 0, j, :], sq[:, :, :], AX.X, ALU.add).then_inc(t1_ss, 1)
                        dve.wait_ge(t1_ss, n + 1)
                        dve.tensor_scalar(qk_st[:, 1, j, :], qk_st[:, 0, j, :], 1.0 / P, EPS,
                                          ALU.mult, ALU.add).then_inc(t1_var, 1)
                        dve.wait_ge(t1_rstd, n + 1)
                        dve.wait_ge(t1_gain, n)
                        dve.tensor_tensor(qn[:, :, :], ps, qk_st[:, 2, j, :, None].broadcast_to([P, 4, P]),
                                          ALU.mult).then_inc(t1_norm, 1)
                        dve.wait_ge(t1_gain, n + 1)
                        dve.wait_ge(rot_done, 2 * n)
                        cb = cos_t[:, 4 * (j % 2):4 * (j % 2) + 4, None, :].broadcast_to([P, 4, 2, 64])
                        dve.tensor_tensor(rc[:, :, :].rearrange("p t (a f) -> p t a f", a=2),
                                          qg[:, :, :].rearrange("p t (a f) -> p t a f", a=2), cb,
                                          ALU.mult).then_inc(t1_cos, 1)
                        dve.wait_ge(t1_cos, n + 1)
                        dve.wait_ge(t1_sin, 2 * n + 2)
                        dve.wait_ge(t2_ready, 8 * h + (j - 1 if j >= 2 else 0))
                        dve.tensor_tensor(rot[:, j % 2, :, 0:64], rc[:, :, 0:64], rs[:, :, 0:64],
                                          ALU.subtract).then_inc(rot_done, 1)
                        dve.tensor_tensor(rot[:, j % 2, :, 64:128], rc[:, :, 64:128], rs[:, :, 64:128],
                                          ALU.add).then_inc(rot_done, 1)
                    elif job[0] == "s":
                        if j < NB:
                            dve.wait_ge(s_ready, NB * h + j + 1)
                            dve.wait_ge(pt_ready, NB * h + (j - 1 if j >= 2 else 0))
                            dve.wait_ge(stat_tr, h)
                            alone(dve)
                            for i in range(2):
                                g, _, prev = unit(j, i)
                                lo = 0 if prev else P
                                mask = wide[:, :] if g == 2 else near[:, lo:]
                                u = 2 * j + i
                                dve.tensor_tensor_reduce(sm[:, j % 2, i, lo:], s_ps[:, 2 * P * i + lo:2 * P * i + 2 * P],
                                                         mask, 1.0, -3.0e38, ALU.add, ALU.max,
                                                         stats[:, u:u + 1]).then_inc(masked, 1)
                            dve.wait_ge(masked, NU * h + 2 * j + 2)
                            dve.tensor_scalar(nmax[:, 2 * j:2 * j + 2], stats[:, 2 * j:2 * j + 2], -SCALE, None,
                                              ALU.mult).then_inc(neg_max, 1)
                        if j >= 2:
                            b = j - 2
                            dve.wait_ge(pv_ready, NB * h + b + 1)
                            dve.wait_ge(wb_mul, 3 * h)
                            dve.tensor_copy(u_t[:, 2 * b:2 * b + 2, :],
                                            o_ps[:, 2 * P * (b % 2):2 * P * (b % 2) + 2 * P]
                                            .rearrange("p (u q) -> p u q", u=2)).then_inc(u_done, 1)
            dve.wait_ge(stat_in, 16 * 8 * (h + 1))

            def order(t, g):
                if g == 1:
                    return t.rearrange("c (r jl) -> c jl r", r=4)
                if g == 2:
                    return t.rearrange("c (r il) -> c il r", r=8)
                return t

            def like(t, g):
                if g == 1:
                    return t.rearrange("c (jl r) -> c jl r", r=4)
                if g == 2:
                    return t.rearrange("c (il r) -> c il r", r=8)
                return t

            cs = [0]

            def cstep(ins):
                cs[0] += 1
                ins.then_inc(c_step, 1)
                dve.wait_ge(c_step, 8 * h + cs[0])

            m8 = mm8[:, :]
            cstep(dve.tensor_copy(m8, st8[:, 0, 0, :]))
            for g in (1, 2):
                cstep(dve.tensor_tensor(like(m8, g), order(st8[:, 0, g, :], g), like(m8, g), ALU.max))
            dve.wait_ge(wgt_out, 16 * h)
            for g in range(NG):
                dve.tensor_tensor(like(e8[:, g, :], g), order(st8[:, 0, g, :], g), like(m8, g),
                                  ALU.subtract).then_inc(c_diff, 1)
            for g in range(NG):
                dve.wait_ge(c_exp, 3 * h + g + 1)
                cstep(dve.tensor_tensor(like(z8[:, g, :], g), order(st8[:, 1, g, :], g), like(e8[:, g, :], g),
                                        ALU.mult))
            cstep(dve.tensor_reduce(z8[:, NG, :], z8[:, 0:NG, :].rearrange("c g t -> c t g"), AX.X, ALU.add))
            cstep(dve.reciprocal(z8[:, NG, :], z8[:, NG, :]))
            for g in range(NG):
                dve.tensor_tensor(e8[:, g, :], e8[:, g, :], z8[:, NG, :], ALU.mult).then_inc(c_wgt, 1)
            dve.wait_ge(wb_in, 16 * h + 16)
            dve.wait_ge(u_done, NB * h + NB)
            for g in range(NG):
                ut = u_t[:, 8 * g:8 * g + 8, :]
                if g == 0:
                    w_, u_ = wb[:, 0, :].rearrange("p (u q) -> p u q", u=8), ut
                elif g == 1:
                    w_ = wb[:, 1, :].rearrange("p (b j r) -> p b j r", b=2, r=4)
                    u_ = ut.rearrange("p (r b) j -> p b j r", b=2)
                else:
                    w_ = wb[:, 2, :].rearrange("p (i r) -> p i r", r=8)
                    u_ = ut.rearrange("p r i -> p i r")
                dve.tensor_tensor(w_, w_, u_, ALU.mult).then_inc(wb_mul, 1)
        leave_phase(dve)
        enter_phase(dve, 2)

        dve.wait_ge(pool_const, 8 + 24)
        def dve_head(h, tail):
            def dve_z(xh):
                n = 2 * h + xh
                dve.wait_ge(z_abs, n + 1)
                dve.wait_ge(b_done, 8 * h + 4 * xh)
                dve.wait_ge(up_copied, 2 * h + 2)
                dve.tensor_scalar(zm[:, :], o_ps, b_a_h[:, 0:1], 0.0, ALU.add, ALU.min).then_inc(z_min, 1)
                dve.wait_ge(z_min, n + 1)
                dve.wait_ge(z_ln, 2 * n + 2)
                if xh == 0:
                    dve.wait_ge(el_done, 4 * h)
                    dve.wait_ge(d_done, 64 * h)
                for c in range(4):
                    cols = slice(HALF * xh + P * c, HALF * xh + P * c + P)
                    dve.tensor_tensor_scan(bcum[:, cols], zm[:, P * c:P * c + P], za[:, P * c:P * c + P], 0.0,
                                           ALU.add, ALU.subtract).then_inc(b_done, 1)

            def dve_f(p):
                cols = slice(2 * P * p, 2 * P * p + 2 * P)
                if p == 0:
                    dve.wait_ge(st_evac, 2 * B0 + 2 * TB * h + 3)
                if p == 2:
                    dve.wait_ge(st_evac, 2 * B0 + 2 * TB * h + 4)
                dve.wait_ge(kh_ready, 8 * h + (2 * (p - 1) if p >= 2 else 0))
                for lv in range(7):
                    m = 64 >> lv
                    dve.wait_ge(e_done, 36 * h + 9 * p + lv + 1)
                    fv, ev, kv, qv = (t.rearrange("p (n two m) -> p n two m", two=2, m=m) for t in
                                      (fbuf[:, p % 2, lv, :], dbuf[:, lv, :], kf[:, cols], qf[:, cols]))
                    dve.tensor_tensor(fv[:, :, 0, :], kv[:, :, 0, :], ev[:, :, 0, :], ALU.mult)
                    dve.tensor_tensor(fv[:, :, 1, :], qv[:, :, 1, :], ev[:, :, 1, :], ALU.mult).then_inc(f_done, 1)
                dve.wait_ge(e_done, 36 * h + 9 * p + 8)
                dve.tensor_tensor(fbuf[:, p % 2, 7, :], kf[:, cols], dbuf[:, 7, :], ALU.mult).then_inc(f_done, 1)
                dve.wait_ge(e_done, 36 * h + 9 * p + 9)
                t = qh[:, cols]
                dve.tensor_tensor(t, qf[:, cols], t, ALU.mult).then_inc(f_done, 1)

            def dve_l(c):
                n = 8 * h + c
                dve.wait_ge(l_ready, n + 1)
                dve.wait_ge(att_done, n)
                for b in range(2):
                    dve.tensor_tensor(lvm[:, 4 * b:4 * b + 4, :],
                                      lvl_ps[:, b, :].rearrange("p (l t) -> p l t", t=P),
                                      gmask[:, 4 * b:4 * b + 4, :], ALU.mult).then_inc(l_mask, 1)
                dve.wait_ge(l_mask, 2 * n + 2)
                if c == 0:
                    dve.wait_ge(kv_ready, 8 * h)
                dve.tensor_reduce(att[:, c, :], lvm[:, :, :].rearrange("p l t -> p t l"), AX.X,
                                  ALU.add).then_inc(att_done, 1)

            for s in range(2 * TB):
                k, xh = s // 2, s % 2
                if xh == 0:
                    lo_tile(B0 + TB * h + k + 2, k + 2)
                for kind, j, jh in jobs_b(s, h, tail):
                    if kind == "z":
                        dve_z(j)
                    elif kind == "l":
                        dve_l(j)
                    elif kind == "m":
                        dve_m(jh, j)
                if s in F_AFTER:
                    dve_f(F_AFTER[s])
                if tail and s == 4:
                    dve_gate(h - 1)

        F_AFTER = {2: 0, 3: 1, 5: 2, 7: 3}

        def dve_m(h, c):
            n = 8 * h + c
            dve.wait_ge(o_sq, n + 1)
            if c == 0:
                dve.tensor_copy(state[:, 1, :], ok_ps[:, DV:2 * DV]).then_inc(state_done, 1)
            else:
                dve.wait_ge(state_done, n)
                dve.wait_ge(el_done, 4 * h + c // 2 + 1)
                dve.scalar_tensor_tensor(out=state[:, (c + 1) % 2, :], in0=state[:, c % 2, :],
                                         scalar=elast[:, c:c + 1], in1=ok_ps[:, DV:2 * DV],
                                         op0=ALU.mult, op1=ALU.add).then_inc(state_done, 1)
            dve.tensor_scalar(ost[:, 1, c:c + 1], ost[:, 0, c:c + 1], 1.0 / DV, EPS,
                              ALU.mult, ALU.add).then_inc(o_var, 1)

        def dve_gate(h):
            dve.wait_ge(g_done, h + 1)
            for j in range(4):
                e, xh = j // 2, j % 2
                dve.wait_ge(obt_evac, 8 * h + 4 * xh + 4)
                t = ob_t[:, e, HALF * xh:HALF * xh + HALF]
                dve.scalar_tensor_tensor(out=t, in0=t, scalar=gn[:, e:e + 1],
                                         in1=g_t[:, e, HALF * xh:HALF * xh + HALF], op0=ALU.mult,
                                         op1=ALU.mult).then_inc(ob_gated, 1)

        dve_head(0, False)
        with dve.Fori(1, H) as h:
            dve_head(h, True)
        for kind, j in rest_b():
            if kind == "m":
                dve_m(H - 1, j)
        dve_gate(H - 1)
        leave_phase(dve)
        enter_phase(dve, 3)

        for i in range(12):
            dve.wait_ge(stage_hi, i + 1)
            hi, lo = (oa_hi[:, i, :], oa_lo[:, i, :]) if i < H else (act_hi[:, i - H, :], act_lo[:, i - H, :])
            dve.tensor_tensor(lo, xk[:, i % 8, :], hi.bitcast(F32), ALU.subtract).then_inc(stage_lo, 1)

        def finish_pair(it, n0, last, make_y):
            for k in range(TC):
                if not (last and k >= 4):
                    lo_tile(n0 + k + 2, k + 2)
                if k in (1, 3):
                    for w in (k - 1, k):
                        make_y(w)
                    for w in (k - 1, k):
                        f, xh = w // 2, w % 2
                        dve.wait_ge(yhi_done, 4 * it + w + 1)
                        dve.tensor_tensor(y_lo[:, f, HALF * xh:HALF * xh + HALF], yf[:, xh, :],
                                          y_hi[:, f, HALF * xh:HALF * xh + HALF].bitcast(F32),
                                          ALU.subtract).then_inc(ylo_done, 1)
                if k == 4:
                    for d in range(16):
                        tt, nh = d // 2, d % 2
                        dve.wait_ge(down_ready, 16 * it + d + 1)
                        t = xk[:, tt, HALF * nh:HALF * nh + HALF]
                        if d == 0:
                            dve.wait_ge(acc_done, 16 * it)
                        dve.tensor_tensor(t, banks[4 + d % 4], t, ALU.add).then_inc(acc_done, 1)

        dve.wait_ge(xk_in, 16)
        with dve.Fori(0, NC_IT) as i:
            def merge(w):
                f, xh = w // 2, w % 2
                dve.wait_ge(mix_ready, 8 * i + 4 * f + xh + 3)
                dve.wait_ge(sig_done, 4 * i + w + 1)
                dve.wait_ge(y_done, 4 * i + w)
                dve.wait_ge(yhi_done, 4 * i + (w - 1 if w >= 2 else 0))
                dve.wait_ge(ylo_done, 4 * i + (w - 1 if w >= 2 else 0))
                dve.tensor_tensor(ya[:, :], banks[xh], gl[:, xh, 0, :], ALU.mult).then_inc(mix_step, 1)
                dve.tensor_tensor(yb[:, :], banks[2 + xh], gl[:, xh, 1, :], ALU.mult).then_inc(mix_step, 1)
                dve.wait_ge(mix_step, 8 * i + 2 * w + 2)
                dve.tensor_tensor(yf[:, xh, :], ya[:, :], yb[:, :], ALU.add).then_inc(y_done, 1)

            finish_pair(i, C0 + TC * i, False, merge)
        leave_phase(dve)
        enter_phase(dve, 4)
        norm_lo(1, xk, xn, gain2)
        leave_phase(dve)
        enter_phase(dve, 5)

        def ffn(i, last):
            it = NC_IT + i

            def swiglu(w):
                f, xh = w // 2, w % 2
                dve.wait_ge(mix_ready, 8 * it + 4 * f + xh + 3)
                dve.wait_ge(sig_done, 4 * it + w + 1)
                dve.wait_ge(yhi_done, 4 * it + (w - 1 if w >= 2 else 0))
                dve.wait_ge(ylo_done, 4 * it + (w - 1 if w >= 2 else 0))
                dve.tensor_tensor(yf[:, xh, :], banks[2 + xh], gl[:, xh, 0, :], ALU.mult).then_inc(y_done, 1)
            finish_pair(it, D0 + TC * i, last, swiglu)

        with dve.Fori(0, ND_IT - 1) as i:
            ffn(i, False)
        ffn(ND_IT - 1, True)

    @block.tensor
    def _(pe):
        def three(ps, lhs_hi, lhs_lo, rhs_hi, rhs_lo, first, last):
            pe.matmul(ps, lhs_hi, rhs_hi, start=first, stop=False)
            pe.matmul(ps, lhs_hi, rhs_lo, start=False, stop=False)
            return pe.matmul(ps, lhs_lo, rhs_hi, start=False, stop=last)

        def stream(ps, k, hi, lo, xh, kts=NK):
            for kt in range(kts):
                cols = slice(P * kt, P * kt + P)
                t = slice(HALF * xh, HALF * xh + HALF)
                mm = three(ps, w_hi[:, slot_of(k), cols], w_lo[:, slot_of(k), cols],
                           hi[:, kt, t], lo[:, kt, t], kt == 0, kt == kts - 1)
            return mm

        def norm_turn(j, xt):
            for g in range(2 * NK):
                xh, kt = g // NK, g % NK
                pe.wait_ge(xn_done, 8 * j + 4 * xh + 4)
                if g >= 8:
                    pe.wait_ge(nt_lo, 16 * j + g - 7)
                for i in range(4):
                    tt = 4 * xh + i
                    mm = pe.transpose(banks[g % 8][:, P * i:P * i + P],
                                      xt[:, tt % xt.shape[1], P * kt:P * kt + P], ident[:, :])
                mm.then_inc(nt_ready, 1)

        pe.wait_ge(pool_const, 5)
        norm_turn(0, xin)
        pe.wait_ge(nt_lo, 16)
        pe.wait_ge(ab_lo_done, 1)
        for xh in range(2):
            for kt in range(NK):
                t = slice(HALF * xh, HALF * xh + HALF)
                mm = three(banks[xh][0:LR, :], ab_hi[:, kt, :], ab_lo[:, kt, :], act_hi[:, kt, t],
                           act_lo[:, kt, t], kt == 0, kt == NK - 1)
            mm.then_inc(ab_ready, 1)
        leave_phase(pe)
        enter_phase(pe, 1)

        with pe.Fori(0, H) as h:
            def x_bank(job):
                at = X_ORDER.index(job)
                if at < 2:
                    pe.wait_ge(t2_evac, 8 * h)
                else:
                    kind, j = X_ORDER[at - 2][0], int(X_ORDER[at - 2][1:])
                    if kind == "v":
                        pe.wait_ge(v_evac, 6 * h + j + 1)
                    elif kind == "a":
                        pe.wait_ge(t1_norm, 8 * h + j + 1)
                    else:
                        pe.wait_ge(t2_evac, 8 * h + j + 1)
                return x_ps[at % 2]

            def pe_s(b):
                if b == 0:
                    pe.wait_ge(neg_max, NB * h)
                else:
                    pe.wait_ge(neg_max, NB * h + b)
                need = {0: 3, 2: 4, 4: 6, 8: 8}
                if b in need:
                    pe.wait_ge(t2_evac, 8 * h + need[b])
                for i in range(2):
                    g, n, prev = unit(b, i)
                    q = tokens(qk_t[:, 1 + g, :], g, n)
                    o = s_ps[:, 2 * P * i:2 * P * i + 2 * P]
                    if g == 0:
                        kk = qk_t[:, 0, P * (n - prev):P * n + P]
                    elif g == 1:
                        r = n // 2
                        kk = qk_t[:, 0, r:r + (8 if prev else 4) * P - 3:4]
                    else:
                        kk = tokens(qk_t[:, 0, :], g, n)
                    mm = pe.matmul(o if prev else o[:, P:], q, kk, start=True, stop=True)
                mm.then_inc(s_ready, 1)

            def pe_t(b):
                pe.wait_ge(p_done, NU * h + 2 * b + 2)
                if b == 0:
                    pe.wait_ge(stat_sbd, h)
                pe.wait_ge(pt_evac, NB * h + b)
                for i in range(2):
                    _, _, prev = unit(b, i)
                    for kb in range(0 if prev else 1, 2):
                        at = P * (2 * i + kb)
                        mm = pe.transpose(pt_ps[:, at:at + P], sm[:, b % 2, i, P * kb:P * kb + P], ident[:, :])
                mm.then_inc(pt_ready, 1)

            def pe_pv(b):
                pe.wait_ge(pt_evac, NB * h + b + 1)
                if b == 0:
                    pe.wait_ge(v_evac, 6 * h + 6)
                pe.wait_ge(u_done, NB * h + b)
                for i in range(2):
                    g, n, prev = unit(b, i)
                    o = o_ps[:, P * (2 * (b % 2) + i):P * (2 * (b % 2) + i) + P]
                    u = 8 * g + n
                    if prev:
                        pe.matmul(o, vt[:, u - 1, :], pt[:, b % 2, i, 0, :], start=True, stop=False)
                    mm = pe.matmul(o, vt[:, u, :], pt[:, b % 2, i, 1, :], start=not prev, stop=True)
                mm.then_inc(pv_ready, 1)

            for s in range(2 * TA):
                k, xh = s // 2, s % 2
                if xh == 0:
                    pe.wait_ge(lo_done, TA * h + k + 1)
                pe.wait_ge(st_evac, 2 * TA * h + (s - 1 if s else 0))
                stream(banks[xh], k, act_hi, act_lo, xh).then_inc(st_ready, 1)
                for job in JOBS_A.get(s, []):
                    j = int(job[1:])
                    if job[0] == "v":
                        ps = x_bank(job)
                        pe.wait_ge(st_evac, 2 * TA * h + (1 if j == 0 else 2))
                        for i in range(4):
                            u = 4 * j + i
                            mm = pe.transpose(ps[:, P * i:P * i + P], tokens(v_raw[:, :], u // 8, u % 8), ident[:, :])
                        mm.then_inc(vtr_ready, 1)
                    elif job[0] == "a":
                        ps = x_bank(job)
                        pe.wait_ge(st_evac, 2 * TA * h + j + 3)
                        for i in range(4):
                            mm = pe.transpose(ps[:, P * i:P * i + P], qk_raw[:, j % 2, P * i:P * i + P], ident[:, :])
                        mm.then_inc(t1_ready, 1)
                    elif job[0] == "b":
                        ps = x_bank(job)
                        pe.wait_ge(rot_done, 16 * h + 2 * j + 2)
                        for i in range(4):
                            mm = pe.transpose(ps[:, P * i:P * i + P], rot[:, j % 2, i, :], ident[:, :])
                        mm.then_inc(t2_ready, 1)
                    else:
                        if j < NB:
                            pe_s(j)
                        if 1 <= j <= NB:
                            pe_t(j - 1)
                        if j >= 2:
                            pe_pv(j - 2)
            pe.wait_ge(p_done, NU * h + NU)
            pe.wait_ge(pt_evac, NB * h + NB)
            alone(pe)
            pe.transpose(pt_ps[0:2 * NU, 0:P], stats[:, :], ident[:, :]).then_inc(stat_tr, 1)
        leave_phase(pe)
        enter_phase(pe, 2)

        def pe_head(h, tail):
            base = 2 * B0 + 2 * TB * h

            def pe_z(xh):
                n = 2 * h + xh
                if xh == 0:
                    pe.wait_ge(up_copied, 2 * h + 2)
                pe.wait_ge(z_abs, n)
                pe.wait_ge(z_min, n)
                pe.matmul(o_ps, w_up_h[:, :], ab_t[:, HALF * xh:HALF * xh + HALF], start=True,
                          stop=True).then_inc(z_ready, 1)

            def pe_v(j):
                pe.wait_ge(st_evac, base + 4 + j + 1)
                if j == 0:
                    pe.wait_ge(obt_evac, 8 * h)
                else:
                    pe.wait_ge(vb_evac, 4 * h + j)
                for i in range(4):
                    mm = pe.transpose(bank3[:, P * i:P * i + P], raw2[:, j % 2, P * i:P * i + P], ident[:, :])
                mm.then_inc(vb_ready, 1)

            def pe_l(c):
                p, cols = c // 2, slice(P * (c % 2), P * (c % 2) + P)
                n = 8 * h + c
                pe.wait_ge(f_done, 36 * h + 9 * p + 9)
                if c % 4 == 0:
                    pe.wait_ge(st_evac, base + 3 + c // 4)
                pe.wait_ge(l_mask, 2 * n)
                for lv in range(7):
                    t = fbuf[:, p % 2, lv, cols]
                    pe.matmul(lvl_ps[:, lv // 4, P * (lv % 4):P * (lv % 4) + P], t, t, start=True, stop=True)
                ct = slice(P * c, P * c + P)
                pe.matmul(lvl_ps[:, 1, 3 * P:4 * P], kf[:, ct], qf[:, ct], start=True, stop=True
                          ).then_inc(l_ready, 1)
                pe.wait_ge(kh_evac, 8 * h + c)
                pe.transpose(s_ps[:, P * (c % 4):P * (c % 4) + P], fbuf[:, p % 2, 7, cols], ident[:, :]
                             ).then_inc(kh_ready, 1)

            for s in range(2 * TB):
                k, xh = s // 2, s % 2
                if xh == 0:
                    pe.wait_ge(lo_done, B0 + TB * h + k + 1)
                pe.wait_ge(st_evac, base + (s - 1 if s else 0))
                stream(banks[xh], k, act_hi, act_lo, xh).then_inc(st_ready, 1)
                for kind, j, jh in jobs_b(s, h, tail):
                    if kind == "z":
                        pe_z(j)
                    elif kind == "v":
                        pe_v(j)
                    elif kind == "l":
                        pe_l(j)
                    else:
                        (pe_m if kind == "m" else pe_t)(jh, j)

        def pe_m(h, c):
            n = 8 * h + c
            p, cols = c // 2, slice(P * (c % 2), P * (c % 2) + P)
            pe.wait_ge(att_done, n + 1)
            pe.wait_ge(kh_evac, n + 1)
            pe.wait_ge(vb_evac, 4 * h + 3 + c // 4)
            pe.wait_ge(obn_done, n)
            pe.wait_ge(state_done, n)
            pe.matmul(ok_ps[:, 0:DV], att[:, c, :], vtok[:, c, :], start=True, stop=(c == 0))
            if c:
                pe.matmul(ok_ps[:, 0:DV], qh[:, P * c:P * c + P], state[:, c % 2, :], start=False, stop=True)
            pe.matmul(ok_ps[:, DV:2 * DV], khat[:, c, :], vtok[:, c, :], start=True, stop=True
                      ).then_inc(kv_ready, 1)

        def pe_t(h, c):
            pe.wait_ge(obn_done, 8 * h + c + 1)
            pe.wait_ge(obt_evac, 8 * h + c)
            pe.wait_ge(vb_evac, 4 * h + 4)
            for e in range(2):
                mm = pe.transpose(bank3[:, P * e:P * e + P], obn[:, c % 2, P * e:P * e + P], ident[:, :])
            mm.then_inc(obt_ready, 1)

        pe_head(0, False)
        with pe.Fori(1, H) as h:
            pe_head(h, True)
        for kind, j in rest_b():
            (pe_m if kind == "m" else pe_t)(H - 1, j)
        leave_phase(pe)
        enter_phase(pe, 3)

        def pair(it, n0, src_a, src_b, kts_a):
            for k in range(4):
                f = k // 2
                pe.wait_ge(lo_done, n0 + k + 1)
                for xh in range(2):
                    w = 2 * f + xh
                    if k % 2 == 0:
                        pe.wait_ge(y_done, 4 * it + (w - 1 if w >= 2 else 0))
                        stream(banks[xh], k, *src_a, xh, kts_a).then_inc(mix_ready, 1)
                    else:
                        stream(banks[2 + xh], k, *src_b, xh).then_inc(mix_ready, 1)
            pe.wait_ge(lo_done, n0 + TC)
            for d in range(16):
                tt, nh = d // 2, d % 2
                if d % 8 == 0:
                    pe.wait_ge(ylo_done, 4 * it + 3 + d // 8)
                pe.wait_ge(acc_done, 16 * it + (d - 3 if d >= 4 else 0))
                cols = slice(P * tt, P * tt + P)
                for kt in range(2):
                    out = slice(HALF * nh, HALF * nh + HALF)
                    mm = three(banks[4 + d % 4], y_hi[:, kt, cols], y_lo[:, kt, cols],
                               w_hi[:, slot_of(4 + kt), out], w_lo[:, slot_of(4 + kt), out], kt == 0, kt == 1)
                mm.then_inc(down_ready, 1)

        pe.wait_ge(stage_lo, 12)
        with pe.Fori(0, NC_IT) as i:
            pair(i, C0 + TC * i, (oa_hi, oa_lo), (act_hi, act_lo), H)
        leave_phase(pe)
        enter_phase(pe, 4)
        norm_turn(1, xn)
        leave_phase(pe)
        enter_phase(pe, 5)
        pe.wait_ge(nt_lo, 32)
        with pe.Fori(0, ND_IT) as i:
            pair(NC_IT + i, D0 + TC * i, (act_hi, act_lo), (act_hi, act_lo), NK)

    ctx.close()


_INS = ["x", "positions", "norm1", "w_in", "qn_a", "kn_a", "w_a_up", "b_a", "gn_b", "w_proj_a", "w_proj_b",
        "w_out", "norm2", "w_ffn_gate", "w_ffn_up", "w_ffn_down"]


def kernel(**inputs):
    import numpy as np
    import concourse.bacc as bacc
    from concourse.bass_utils import run_bass_kernel_spmd

    nc = bacc.Bacc("TRN2", target_bir_lowering=False, num_devices=1)
    arrays = {f"in_{n}": np.ascontiguousarray(inputs[n]) for n in _INS}
    arrays["in_inv_freq"] = (10000.0 ** (-np.arange(0, 128, 2) / 128)).astype(np.float32)
    args = [nc.dram_tensor(n, a.shape, mybir.dt.from_np(a.dtype), kind="ExternalInput").ap()
            for n, a in arrays.items()]
    out = nc.dram_tensor("out_y", inputs["x"].shape, F32, kind="ExternalOutput").ap()
    decoder_layer(nc, *args, out)
    r = run_bass_kernel_spmd(nc, [arrays], core_ids=[0])
    return r.results[0]["out_y"]
```

```python
from contextlib import ExitStack

import concourse.bass as bass
from concourse import mybir

F32 = mybir.dt.float32
F32R = mybir.dt.float32r
I32 = mybir.dt.int32
ALU = mybir.AluOpType
ACT = mybir.ActivationFunctionType
AX = mybir.AxisListType

P = 128
HALF = 512
NEG = -1.0e30
TWO_PI = 6.283185307179586
ROUND = 12582912.0
PI_C1 = 6.28125
PI_C2 = 0.0019340515136718750
PI_C3 = TWO_PI - PI_C1 - PI_C2
PI_SAFE = 3.1415925


def decoder_layer(nc, x_d, pos_d, norm1_d, w_in_d, qn_d, kn_d, w_up_d, b_a_d, gn_d, w_pa_d, w_pb_d,
                  w_out_d, norm2_d, w_fg_d, w_fu_d, w_fd_d, inv_freq_d, out_d):
    S, D = x_d.shape[1], x_d.shape[2]
    NT = S // P
    NK = D // P
    FF = w_fg_d.shape[2]
    LR = w_up_d.shape[1]
    H = 4
    NG = 3
    DV = gn_d.shape[1]
    W_Q, W_KV, W_B = NG * H * P, H * P, H * P
    C_K = W_Q
    C_V = C_K + W_KV
    C_QB = C_V + W_KV
    C_KB = C_QB + W_B
    C_VB = C_KB + W_B
    C_RB = C_VB + H * DV
    C_AB = C_RB + H * DV
    C_G = C_AB + LR
    SCALE = float(P) ** -0.5
    EPS = 1e-6
    TEMP = 16.0
    assert S == 1024 and D == 1024 and DV == 256 and C_G + 2 * D == w_in_d.shape[2]

    TA, TB, TC = 9, 6, 6
    A0, B0, C0 = 0, H * TA, H * (TA + TB)
    NC_IT = D // (2 * P)
    D0 = C0 + NC_IT * TC
    ND_IT = FF // (2 * P)
    NU = NG * 8
    NB = NU // 2
    LV = 8

    w_in = w_in_d[0].rearrange("(kt p) n -> p kt n", p=P)
    w_pa = w_pa_d[0].rearrange("(kt p) n -> p kt n", p=P)
    w_pb = w_pb_d[0].rearrange("(kt p) n -> p kt n", p=P)
    w_fg = w_fg_d[0].rearrange("(kt p) n -> p kt n", p=P)
    w_fu = w_fu_d[0].rearrange("(kt p) n -> p kt n", p=P)
    w_out = w_out_d[0]
    w_fd = w_fd_d[0]
    x_t = x_d[0].rearrange("(tt p) d -> p tt d", p=P)
    out_t = out_d[0].rearrange("(tt p) d -> p tt d", p=P)

    gate_d = nc.dram_tensor("gate_scratch", (2 * NK, P, S), F32).ap()
    stat_d = nc.dram_tensor("stat_scratch", (H, 2 * NU, P), F32).ap()
    wgt_d = nc.dram_tensor("weight_scratch", (H, NG, NT, P), F32).ap()
    oa_d = nc.dram_tensor("oa_scratch", (H, P, S), F32).ap()
    ob_d = nc.dram_tensor("ob_scratch", (2 * H, P, S), F32).ap()

    ctx = ExitStack()

    def sem(name):
        return ctx.enter_context(nc.semaphore(name))

    def on(stack):
        def sb(name, shape, dt=F32):
            return stack.enter_context(nc.sbuf_tensor(name, shape, dt))
        return sb

    sb = on(ctx)
    act_hi = sb("act_hi", [P, NK, S], F32R)
    act_lo = sb("act_lo", [P, NK, S], F32R)
    w_raw = sb("w_raw", [P, 3, 1024])
    w_hi = sb("w_hi", [P, 3, 1024], F32R)
    w_lo = sb("w_lo", [P, 3, 1024], F32R)
    ident = sb("ident", [P, P])
    small = sb("small", [P, 128])
    gain1, gain2 = small[:, 0:8], small[:, 8:16]
    ssq, var, rstd = small[:, 16:24], small[:, 24:32], small[:, 32:40]
    b_a = small[:, 40:44]
    gn = small[:, 44:46]
    elast = small[:, 56:64]
    ost = small[:, 64:88].rearrange("p (a c) -> p a c", a=3)
    b_a_h = small[:, 88:89]
    mhalf = small[:, 48:56]
    w_up = sb("w_up", [2 * LR, H * P])
    ab_t = sb("ab_t", [2 * LR, S])

    with ExitStack() as mem:
        sb = on(mem)
        cos_t = sb("cos_t", [P, NT, 64])
        sin_t = sb("sin_t", [P, NT, 64])
        q_gain = sb("q_gain", [P, P])
        k_gain = sb("k_gain", [P, P])
        near = sb("near", [P, 2 * P])
        wide = sb("wide", [P, P])
        u_t = sb("u_t", [P, NU, P])
        wb = sb("wb", [P, NG, S])
        e8 = sb("e8", [NT, NG, P])
        z8 = sb("z8", [NT, NG + 1, P])
        mm8 = sb("mm8", [NT, P])
        st8 = sb("st8", [NT, 2, NG, P])
        stat_sb = sb("stat_sb", [2 * NU, P])
        v_raw = sb("v_raw", [P, S])
        qk_raw = sb("qk_raw", [P, 2, HALF])
        qg = sb("qg", [P, 4, P])
        rc = sb("rc", [P, 4, P])
        rs = sb("rs", [P, 4, P])
        rot = sb("rot", [P, 2, 4, P])
        qk_st = sb("qk_st", [P, 3, 8, 4])
        qk_t = sb("qk_t", [P, 4, S])
        vt = sb("vt", [P, NU, P])
        sm = sb("sm", [P, 3, 2, 2 * P])
        pt = sb("pt", [P, 2, 2, 2, P])
        nmax = sb("nmax", [P, NU])
        stats = sb("stats", [P, 2 * NU])
        gbuf = sb("gbuf", [P, 2, HALF])
    with ExitStack() as mem:
        sb = on(mem)
        hold = sb("hold", [P, NT * 64 * 2 + 4 * P + P])
        xin = sb("xin", [P, NT, D])
        junk = sb("junk", [P, D])
        ang = sb("ang", [P, NT, 64])
        tra = sb("tra", [P, NT, 64])
        trb = sb("trb", [P, NT, 64])
        red = sb("red", [P, NT, 64])
        posi = sb("posi", [P, NT], I32)
        posf = sb("posf", [P, NT])
        invf = sb("invf", [P, 64])
        ab_raw = sb("ab_raw", [P, NK, LR])
        ab_w = sb("ab_w", [P, NK, 2 * LR], F32R)
        pari = sb("pari", [P, P], I32)
        parj = sb("parj", [P, P], I32)
        parf = sb("parf", [P, P])
    with ExitStack() as mem:
        sb = on(mem)
        gmask = sb("gmask", [P, LV, P])
        w_up_h = sb("w_up_h", [2 * LR, P])
        zm = sb("zm", [P, HALF])
        g_t = sb("g_t", [P, 2, S])
        ob_t = sb("ob_t", [P, 2, S])
        state = sb("state", [P, 2, DV])
        obn = sb("obn", [P, 2, DV])
        osq = sb("osq", [P, DV])
        sb("rest_of_wb", [P, NG * S + NU * P - 4 * S - 5 * DV])
        vtok = sb("vtok", [P, NT, DV])
        att = sb("att", [P, NT, P])
        khat = sb("khat", [P, NT, P])
        qh = sb("qh", [P, S])
        to_tail = LV * P + P + HALF + NG * S + NU * P + NT * DV + 3 * S
        bcum = sb("bcum", [P, S])
        za = sb("za", [P, HALF])
        raw2 = sb("raw2", [P, 2, HALF])
        dbuf = sb("dbuf", [P, 8, 2 * P])
        fbuf = sb("fbuf", [P, 2, 8, 2 * P])
        kf = sb("kf", [P, S])
        qf = sb("qf", [P, S])
        lvm = sb("lvm", [P, LV, P])
    with ExitStack() as mem:
        sb = on(mem)
        hold3 = sb("hold3", [P, to_tail])
        stage = sb("stage", [P, 4, S])
    with ExitStack() as mem:
        sb = on(mem)
        xk = sb("xk", [P, NT, D])
        gl = sb("gl", [P, 2, 2, HALF])
        y_hi = sb("y_hi", [P, 2, S], F32R)
        y_lo = sb("y_lo", [P, 2, S], F32R)
        ya = sb("ya", [P, HALF])
        yb = sb("yb", [P, HALF])
        yf = sb("yf", [P, 2, HALF])
        sb("rest_of_stage", [P, to_tail + 4 * S - NT * D - 4 * S - 2 * S - 4 * HALF])
        oa_hi = sb("oa_hi", [P, H, S], F32R)
        oa_lo = sb("oa_lo", [P, H, S], F32R)
    with ExitStack() as mem:
        sb = on(mem)
        hold2 = sb("hold2", [P, to_tail + 4 * S])
        xn = sb("xn", [P, NT, D])

    bank = [ctx.enter_context(nc.psum_tensor(f"bank{i}", [P, HALF], F32)) for i in range(5)]
    lvl_ps = ctx.enter_context(nc.psum_tensor("lvl_ps", [P, 2, HALF], F32))
    bank7 = ctx.enter_context(nc.psum_tensor("bank7", [P, HALF], F32))
    banks = [*(b[:, :] for b in bank), lvl_ps[:, 0, :], lvl_ps[:, 1, :], bank7[:, :]]
    s_ps, pt_ps, o_ps = banks[2], banks[3], banks[4]
    score_ps = [banks[2], banks[7]]
    x_ps = [banks[5], banks[6]]
    ok_ps = banks[7]
    bank3 = banks[3]

    phase_end = sem("phase_end")
    raw_in = [sem(f"raw_in{i}") for i in range(3)]
    hi_done, lo_done = sem("hi_done"), sem("lo_done")
    x_in = [sem(f"x_in{i}") for i in range(NT)]
    gain_in, pos_in, const_in = sem("gain_in"), sem("pos_in"), sem("const_in")
    passed = sem("passed")
    pool_const = sem("pool_const")
    par_done = sem("par_done")
    pos_step = sem("pos_step")
    sin_done = sem("sin_done")
    ssq_done, var_done, rstd_done, xn_done = sem("ssq_done"), sem("var_done"), sem("rstd_done"), sem("xn_done")
    nt_ready, nt_hi, nt_lo = sem("nt_ready"), sem("nt_hi"), sem("nt_lo")
    ab_hi_done, ab_lo_done = sem("ab_hi_done"), sem("ab_lo_done")
    ab_ready, ab_done = sem("ab_ready"), sem("ab_done")
    ab_in = sem("ab_in")
    st_ready, st_evac = sem("st_ready"), sem("st_evac")
    gate_out = [sem("gate_out0"), sem("gate_out1")]
    vtr_ready, v_evac = sem("vtr_ready"), sem("v_evac")
    t1_ready, t1_sq, t1_ss, t1_var, t1_rstd = (sem("t1_" + n) for n in ("ready", "sq", "ss", "var", "rstd"))
    t1_gain, t1_cos, t1_sin, rot_done = sem("t1_gain"), sem("t1_cos"), sem("t1_sin"), sem("rot_done")
    t2_ready, t2_evac = sem("t2_ready"), sem("t2_evac")
    s_ready, masked, neg_max, p_done = sem("s_ready"), sem("masked"), sem("neg_max"), sem("p_done")
    pt_ready, pt_evac, pv_ready, u_done = sem("pt_ready"), sem("pt_evac"), sem("pv_ready"), sem("u_done")
    stat_tr, stat_sbd, stat_out, stat_in = sem("stat_tr"), sem("stat_sbd"), sem("stat_out"), sem("stat_in")
    c_step, c_diff, c_exp, c_wgt = sem("c_step"), sem("c_diff"), sem("c_exp"), sem("c_wgt")
    wgt_out, wb_in, wb_mul, wb_sum, oa_out = (sem(n) for n in ("wgt_out", "wb_in", "wb_mul", "wb_sum", "oa_out"))
    up_copied, z_ready, z_abs, z_min, z_ln, b_done = (sem(n) for n in
                                                      ("up_copied", "z_ready", "z_abs", "z_min", "z_ln", "b_done"))
    d_done, e_done, f_done, el_done = sem("d_done"), sem("e_done"), sem("f_done"), sem("el_done")
    vb_ready, vb_evac = sem("vb_ready"), sem("vb_evac")
    g_done = sem("g_done")
    l_ready, l_mask, att_done = sem("l_ready"), sem("l_mask"), sem("att_done")
    kh_ready, kh_evac = sem("kh_ready"), sem("kh_evac")
    kv_ready, state_done = sem("kv_ready"), sem("state_done")
    o_sq, o_var, o_rstd, obn_done = sem("o_sq"), sem("o_var"), sem("o_rstd"), sem("obn_done")
    obt_ready, obt_evac, ob_gated, ob_out = sem("obt_ready"), sem("obt_evac"), sem("ob_gated"), sem("ob_out")
    stage_in = [sem(f"stage_in{i}") for i in range(4)]
    stage_hi, stage_lo = sem("stage_hi"), sem("stage_lo")
    xk_in = [sem("xk_in0"), sem("xk_in1")]
    gl_in = [sem("gl_in0"), sem("gl_in1")]
    sig_done = sem("sig_done")
    mix_ready, mix_step, y_done, yhi_done, ylo_done = (sem(n) for n in
                                                       ("mix_ready", "mix_step", "y_done", "yhi_done", "ylo_done"))
    down_ready, acc_done = sem("down_ready"), sem("acc_done")
    out_done = sem("out_done")

    block = ctx.enter_context(nc.Block())

    def enter_phase(eng, k):
        eng.wait_ge(phase_end, 4 * k)

    def alone(eng):
        eng.sem_inc(passed, 1)

    def leave_phase(eng):
        eng.drain().then_inc(phase_end, 1)

    JOBS_A = {2: ["v0", "v1"], 3: ["v2", "a0"], 4: ["v3", "a1"], 5: ["v4", "a2", "b0"],
              6: ["v5", "a3", "b1"], 7: ["a4", "b2"], 8: ["a5", "b3", "s0"], 9: ["s1", "a6", "b4"],
              10: ["s2", "a7", "b5"], 11: ["s3", "b6"], 12: ["s4", "s5", "b7"], 13: ["s6", "s7"],
              14: ["s8", "s9"], 15: ["s10", "s11"], 16: ["s12", "s13"], 17: ["s14"]}
    X_ORDER = [j for s in sorted(JOBS_A) for j in JOBS_A[s] if j[0] in "vab"]
    JOBS_B = {0: ["z0"], 1: ["z1"], 4: ["l0"], 5: ["v0", "l1"], 6: ["v1", "l2"], 7: ["v2", "l3"],
              8: ["v3", "m0", "l4"], 9: ["t0", "m1", "l5"], 10: ["t1", "m2", "l6"], 11: ["t2", "m3", "l7"]}
    TAIL_B = {0: ["t3", "m4"], 1: ["t4", "m5"], 2: ["t5", "m6"], 3: ["t6", "m7"], 4: ["t7"]}

    def jobs_b(s, h, tail):
        own = [(j[0], int(j[1:]), h) for j in JOBS_B.get(s, [])]
        old = [(j[0], int(j[1:]), h - 1) for j in TAIL_B.get(s, [])] if tail else []
        return old + own if s == 4 else own + old

    def rest_ps(c):
        return banks[4] if c % 2 else banks[7]

    N_ST = H + 2 * (H - 1)

    def slot_of(k):
        return k % 3

    def unit(b, i):
        u = 2 * b + i
        g, n = u // 8, u % 8
        return g, n, (g == 0 and n > 0) or (g == 1 and n % 2 == 1)

    def tokens(t, g, n):
        if g == 0:
            return t[:, P * n:P * n + P]
        if g == 1:
            r, b = n // 2, n % 2
            return t[:, 4 * P * b + r:4 * P * b + r + 4 * P - 3:4]
        return t[:, n:n + 8 * P - 7:8]

    @block.sync
    def _(sp):
        for i in range(NT):
            sp.dma_start(xin[:, i, :], x_t[:, i, :]).then_inc(x_in[i], 16)
            if i == 3:
                sp.dma_start(ab_raw[:, :, :], w_in[:, :, C_AB:C_AB + LR]).then_inc(ab_in, 16)

        def load(n, k, src, parts=None):
            dst = w_raw[:, slot_of(k), :] if parts is None else w_raw[:, slot_of(k), 0:parts]
            if len(src.shape) == 3:
                dst = dst.rearrange("p (kt n) -> p kt n", n=P)
            sp.dma_start(dst, src).then_inc(raw_in[slot_of(k)], 16)

        def free(n):
            sp.wait_ge(lo_done, n - 2)
            alone(sp)

        def load_a(h, k):
            cols = [C_V + P * h, C_K + P * h, P * h, W_KV + P * h, 2 * W_KV + P * h,
                    C_G + 4 * P * h, C_G + 4 * P * h + P, C_G + 4 * P * h + 2 * P, C_G + 4 * P * h + 3 * P]
            load(A0 + TA * h + k, k, w_in[:, :, bass.ds(cols[k], P)])

        for k in range(3):
            load_a(0, k)
        for k in range(3, TA):
            free(k)
            load_a(0, k)
        with sp.Fori(1, H) as h:
            for k in range(TA):
                free(A0 + TA * h + k)
                load_a(h, k)
        with sp.Fori(0, H) as h:
            cols = [C_KB + P * h, C_QB + P * h, C_VB + DV * h, C_VB + DV * h + P,
                    C_RB + DV * h, C_RB + DV * h + P]
            for k in range(TB):
                free(B0 + TB * h + k)
                load(B0 + TB * h + k, k, w_in[:, :, bass.ds(cols[k], P)])
        def load_c(i, k):
            free(C0 + TC * i + k)
            f = k // 2
            if k in (0, 2):
                load(0, k, w_pa[:, :, bass.ds(2 * P * i + P * f, P)], parts=H * P)
            elif k in (1, 3):
                load(0, k, w_pb[:, :, bass.ds(2 * P * i + P * f, P)])
            else:
                load(0, k, w_out[bass.ds(2 * P * i + P * (k - 4), P), :])

        def load_output(i):
            src = oa_d[i] if i < H else ob_d[i - H]
            alone(sp)
            sp.dma_start(stage[:, i % 4, :], src).then_inc(stage_in[i % 4], 16)

        load_c(0, 0)
        load_c(0, 1)
        sp.wait_ge(f_done, 36 * H)
        sp.wait_ge(el_done, 4 * H)
        sp.wait_ge(vb_ready, 4 * H)
        sp.wait_ge(oa_out, 16 * H)
        for i in range(4):
            load_output(i)
        load_c(0, 2)
        sp.wait_ge(ob_out, 16 * (H - 1))
        for i in range(4, N_ST):
            sp.wait_ge(stage_lo, i - 3)
            load_output(i)
        for k in range(3, TC):
            load_c(0, k)
        with sp.Fori(1, NC_IT) as i:
            for k in range(TC):
                load_c(i, k)
        with sp.Fori(0, ND_IT) as i:
            for k in range(TC):
                free(D0 + TC * i + k)
                f = k // 2
                if k in (0, 2):
                    load(0, k, w_fg[:, :, bass.ds(2 * P * i + P * f, P)])
                elif k in (1, 3):
                    load(0, k, w_fu[:, :, bass.ds(2 * P * i + P * f, P)])
                else:
                    load(0, k, w_fd[bass.ds(2 * P * i + P * (k - 4), P), :])
        for tt in range(NT):
            sp.wait_ge(acc_done, 16 * (NC_IT + ND_IT - 1) + 2 * tt + 2)
            sp.dma_start(out_t[:, tt, :], xk[:, tt, :]).then_inc(out_done, 16)
        sp.wait_ge(out_done, 16 * NT)

    @block.gpsimd
    def _(pool):
        pool.dma_start(gain1, norm1_d[0].rearrange("(kt p) -> p kt", p=P),
                       allow_slow_non_contiguous=True).then_inc(gain_in, 16)
        pool.memset(ident[:, :], 0.0).then_inc(pool_const, 1)
        pool.wait_ge(pool_const, 1)
        pool.affine_select(out=ident[:, :], in_=ident[:, :], compare_op=ALU.not_equal, fill=1.0, base=0,
                           pattern=[[-1, P]], channel_multiplier=1).then_inc(pool_const, 1)
        pool.memset(mhalf, -0.5).then_inc(pool_const, 1)
        pool.dma_start(posi[:, :], pos_d[0].rearrange("(tt p) -> p tt", p=P),
                       allow_slow_non_contiguous=True).then_inc(pos_in, 16)
        pool.dma_start(invf[:, :], inv_freq_d[:].partition_broadcast(P)).then_inc(pos_in, 16)

        def norm_rstd(j, size):
            for i in range(NT // size):
                cols = slice(size * i, size * i + size)
                pool.wait_ge(var_done, NT * j + size * i + size)
                pool.tensor_tensor(rstd[:, cols], var[:, cols], mhalf[:, 0:size],
                                   ALU.pow).then_inc(rstd_done, size)

        pool.wait_ge(pool_const, 3)
        norm_rstd(0, 1)
        pool.memset(near[:, :], 0.0).then_inc(pool_const, 1)
        pool.iota(pari[:, :], pattern=[[1, P]], base=P, channel_multiplier=-1).then_inc(pool_const, 1)
        pool.wait_ge(pool_const, 4)
        pool.affine_select(out=near[:, :], in_=near[:, :], compare_op=ALU.is_ge, fill=NEG, base=0,
                           pattern=[[1, 2 * P]], channel_multiplier=-1).then_inc(pool_const, 1)
        pool.dma_start(k_gain[:, :], kn_d[0].partition_broadcast(P)).then_inc(const_in, 16)
        pool.dma_start(q_gain[:, :], qn_d[0].partition_broadcast(P)).then_inc(const_in, 16)
        pool.wait_ge(pool_const, 6)
        pool.affine_select(out=near[:, :], in_=near[:, :], compare_op=ALU.is_ge, fill=NEG, base=P,
                           pattern=[[-1, 2 * P]], channel_multiplier=1).then_inc(pool_const, 1)
        pool.dma_start(gain2, norm2_d[0].rearrange("(kt p) -> p kt", p=P),
                       allow_slow_non_contiguous=True).then_inc(const_in, 16)
        pool.dma_start(b_a, b_a_d[0].rearrange("(h p) -> p h", p=P),
                       allow_slow_non_contiguous=True).then_inc(const_in, 16)
        pool.dma_start(gn, gn_d[0].rearrange("(e p) -> p e", p=P),
                       allow_slow_non_contiguous=True).then_inc(const_in, 16)
        for i in range(2):
            pool.dma_start(w_up[LR * i:LR * i + LR, :], w_up_d[0]).then_inc(const_in, 16)
        pool.wait_ge(par_done, 2)
        pool.affine_select(out=wide[:, :], in_=parf[:, :], compare_op=ALU.is_ge, fill=NEG, base=0,
                           pattern=[[-1, P]], channel_multiplier=1).then_inc(pool_const, 1)
        pool.wait_ge(const_in, 16 * 7)
        leave_phase(pool)
        enter_phase(pool, 1)

        def pool_rope(h, j):
            n = 8 * h + j
            pool.wait_ge(t1_var, n + 1)
            pool.tensor_tensor(qk_st[:, 2, j, :], qk_st[:, 1, j, :], mhalf[:, 0:4],
                               ALU.pow).then_inc(t1_rstd, 1)
            pool.wait_ge(t1_gain, 4 * n + 4)
            pool.wait_ge(rot_done, 2 * n)
            sin_b = sin_t[:, 4 * (j % 2):4 * (j % 2) + 4, :]
            pool.tensor_tensor(rs[:, :, 0:64], qg[:, :, 64:128], sin_b, ALU.mult).then_inc(t1_sin, 1)

        def merge_stats(h):
            sd = stat_d[bass.ds(h, 1)].rearrange("a u q -> (a u) q")
            pool.wait_ge(stat_sbd, h + 1)
            alone(pool)
            pool.dma_start(sd, stat_sb[:, :]).then_inc(stat_out, 16)
            pool.wait_ge(stat_out, 16 * h + 16)
            pool.wait_ge(c_wgt, 3 * h)
            alone(pool)
            for q in range(2):
                r0 = NU * q
                pool.dma_start(st8[:, q, 0, :], sd[r0:r0 + 8, :]).then_inc(stat_in, 16)
                for b in range(2):
                    pool.dma_start(st8[4 * b:4 * b + 4, q, 1, :].rearrange("c (r jl) -> c r jl", jl=32),
                                   sd[r0 + 8 + b:r0 + 16:2, :].rearrange("r (jh jl) -> jh r jl", jl=32)
                                   ).then_inc(stat_in, 16)
                pool.dma_start(st8[:, q, 2, :].rearrange("c (r il) -> c r il", il=16),
                               sd[r0 + 16:r0 + 24, :].rearrange("r (ih il) -> ih r il", il=16)
                               ).then_inc(stat_in, 16)

        def merge_weights(h):
            pool.wait_ge(c_wgt, 3 * h + 3)
            alone(pool)
            wd = wgt_d[bass.ds(h, 1)].rearrange("a g c t -> (a g) c t")
            pool.dma_start(wd.rearrange("g c t -> c g t"), e8[:, :, :]).then_inc(wgt_out, 16)
            pool.wait_ge(wgt_out, 16 * h + 16)
            pool.wait_ge(oa_out, 16 * h)
            alone(pool)
            pool.dma_start(wb[:, :, :], wd.rearrange("g c t -> g (c t)").partition_broadcast(P)
                           ).then_inc(wb_in, 16)

        def merge_sum(h):
            pool.wait_ge(wb_mul, 3 * h + 3)
            pool.tensor_tensor(wb[:, 0, :], wb[:, 0, :], wb[:, 1, :], ALU.add).then_inc(wb_sum, 1)
            pool.wait_ge(wb_sum, 2 * h + 1)
            pool.tensor_tensor(wb[:, 0, :], wb[:, 0, :], wb[:, 2, :], ALU.add).then_inc(wb_sum, 1)
            pool.wait_ge(wb_sum, 2 * h + 2)
            alone(pool)
            pool.dma_start(oa_d[bass.ds(h, 1)].rearrange("a p t -> (a p) t"), wb[:, 0, :]).then_inc(oa_out, 16)

        for j in range(8):
            pool_rope(0, j)
        with pool.Fori(1, H) as h:
            merge_stats(h - 1)
            merge_weights(h - 1)
            for j in range(8):
                pool_rope(h, j)
            merge_sum(h - 1)
        leave_phase(pool)
        merge_stats(H - 1)
        enter_phase(pool, 2)

        nm0 = 8
        pool.memset(gmask[:, 0:7, :], 1.0).then_inc(pool_const, 1)
        pool.memset(gmask[:, 7, :], 0.0).then_inc(pool_const, 1)
        pool.wait_ge(pool_const, nm0 + 2)
        for lv in range(7):
            m = 64 >> lv
            v = gmask[:, lv, :].rearrange("p (n two m) -> p n two m", two=2, m=m)
            nblk = P // (2 * m)
            pool.memset(v[:, :, 0, :], 0.0).then_inc(pool_const, 1)
            pool.affine_select(out=v[:, :, 1, :], in_=v[:, :, 1, :], compare_op=ALU.is_ge, fill=0.0, base=0,
                               pattern=[[-2 * m, nblk], [0, m]], channel_multiplier=1).then_inc(pool_const, 1)
        pool.affine_select(out=gmask[:, 7, :], in_=gmask[:, 7, :], compare_op=ALU.not_equal, fill=1.0, base=0,
                           pattern=[[-1, P]], channel_multiplier=1).then_inc(pool_const, 1)
        pool.wait_ge(pool_const, nm0 + 17)
        for lv in range(7):
            m = 64 >> lv
            v = gmask[:, lv, :].rearrange("p (n two m) -> p n two m", two=2, m=m)
            pool.affine_select(out=v[:, :, 1, :], in_=v[:, :, 1, :], compare_op=ALU.is_ge, fill=0.0, base=m - 1,
                               pattern=[[2 * m, P // (2 * m)], [0, m]], channel_multiplier=-1
                               ).then_inc(pool_const, 1)
        def pool_head(h, tail):
            def pool_d(p):
                for lv in range(8):
                    n = 32 * h + 8 * p + lv
                    m = 64 >> lv if lv < 7 else 64
                    if p == 0:
                        pool.wait_ge(f_done, 36 * h)
                        if lv == 0:
                            pool.wait_ge(b_done, 8 * h + 8)
                    else:
                        pool.wait_ge(f_done, 36 * h + 9 * (p - 1) + lv + 1)
                    bp = bcum[:, 2 * P * p:2 * P * p + 2 * P]
                    dst = dbuf[:, lv, :]
                    if lv < 7:
                        bv = bp.rearrange("p (n two m) -> p n two m", two=2, m=m)
                        dv = dst.rearrange("p (n two m) -> p n two m", two=2, m=m)
                        ref = bv[:, :, 0, m - 1:m].broadcast_to([P, P // m, m])
                        pool.tensor_tensor(dv[:, :, 0, :], ref, bv[:, :, 0, :], ALU.subtract).then_inc(d_done, 1)
                        pool.tensor_tensor(dv[:, :, 1, :], bv[:, :, 1, :], ref, ALU.subtract).then_inc(d_done, 1)
                    else:
                        bv = bp.rearrange("p (n m) -> p n m", m=P)
                        dv = dst.rearrange("p (n m) -> p n m", m=P)
                        ref = bv[:, :, P - 1:P].broadcast_to([P, 2, P])
                        pool.tensor_tensor(dv, ref, bv, ALU.subtract).then_inc(d_done, 2)

            last = ["o0", "o1", "o2", "o3"]
            if tail:
                work = ["O4", "O5", "d0", "O6", "d1", "O7", "d2", "G0", "d3"] + last
            else:
                work = ["d0", "W0", "d1", "S0", "d2", "d3"] + last
            for w in work:
                if w[0] == "d":
                    pool_d(int(w[1]))
                elif w[0] == "o":
                    pool_o(h, int(w[1]))
                elif w[0] == "O":
                    pool_o(h - 1, int(w[1]))
                elif w[0] == "W":
                    merge_weights(H - 1)
                elif w[0] == "S":
                    merge_sum(H - 1)
                else:
                    pool_out(h - 1)

        def pool_o(h, c):
            pool.wait_ge(o_var, 8 * h + c + 1)
            pool.tensor_tensor(ost[:, 2, c:c + 1], ost[:, 1, c:c + 1], mhalf[:, 0:1],
                               ALU.pow).then_inc(o_rstd, 1)

        def pool_out(h):
            pool.wait_ge(ob_gated, 4 * h + 4)
            alone(pool)
            pool.dma_start(ob_d[bass.ds(2 * h, 2)].rearrange("e p t -> p e t"), ob_t[:, :, :]
                           ).then_inc(ob_out, 16)

        pool_head(0, False)
        with pool.Fori(1, H) as h:
            pool_head(h, True)
        for c in range(4, 8):
            pool_o(H - 1, c)
        gd = gate_d.rearrange("(ab f) p t -> f p ab t", ab=2)

        def load_gates(i, w):
            f, xh = w // 2, w % 2
            pool.wait_ge(y_done, 4 * i if w < 2 else 4 * i + w - 1)
            alone(pool)
            src = gd[bass.ds(2 * i + f, 1)].rearrange("a p ab t -> (a p) ab t")
            pool.dma_start(gl[:, xh, :, :], src[:, :, HALF * xh:HALF * xh + HALF]).then_inc(gl_in[xh], 16)
        pool.wait_ge(kv_ready, 8 * H)
        load_gates(0, 0)
        load_gates(0, 1)
        leave_phase(pool)
        enter_phase(pool, 3)
        for tt in range(NT):
            if tt == 2:
                load_gates(0, 2)
                load_gates(0, 3)
            pool.dma_start(xk[:, tt, :], x_t[:, tt, :]).then_inc(xk_in[tt // 4], 16)
        with pool.Fori(1, NC_IT) as i:
            for w in range(4):
                load_gates(i, w)
        norm_rstd(1, 4)

    @block.scalar
    def _(act):
        def hi_tile(k, turn, width=1024):
            act.wait_ge(raw_in[slot_of(k)], 16 * turn)
            act.copy(w_hi[:, slot_of(k), 0:width], w_raw[:, slot_of(k), 0:width]).then_inc(hi_done, 1)

        def norm_hi(j, gain):
            def square(tt):
                act.wait_ge(x_in[tt], 16)
                if tt:
                    act.wait_ge(ssq_done, tt)
                act.activation(junk[:, :], xin[:, tt, :], ACT.Square,
                               accum_out=ssq[:, tt:tt + 1]).then_inc(ssq_done, 1)

            if j == 0:
                for tt in range(4):
                    square(tt)
            for g in range(2 * NK):
                xh, kt = g // NK, g % NK
                if j == 0 and g % 2 == 0 and g < NK:
                    square(4 + g // 2)
                if j == 0 and g == 4:
                    act.wait_ge(ab_in, 16)
                    act.copy(ab_w[:, :, 0:LR], ab_raw[:, :, :]).then_inc(ab_hi_done, 1)
                if g == 0 and j == 0:
                    act.wait_ge(gain_in, 16)
                act.wait_ge(nt_ready, 16 * j + g + 1)
                act.activation(act_hi[:, kt, HALF * xh:HALF * xh + HALF], banks[g % 8], ACT.Copy,
                               scale=gain[:, kt:kt + 1]).then_inc(nt_hi, 1)

        act.preload_act_table_set("natural_log_exp_and_others")
        norm_hi(0, gain1)
        hi_tile(0, 1)
        hi_tile(1, 1)
        act.wait_ge(pos_step, 9)
        act.activation(sin_t[:, :, :], tra[:, :, :], ACT.Sin).then_inc(sin_done, 1)
        act.wait_ge(pos_step, 16)
        act.activation(cos_t[:, :, :], trb[:, :, :], ACT.Sin).then_inc(sin_done, 1)
        act.preload_act_table_set("natural_log_exp_and_others")
        act.wait_ge(ab_ready, 2)
        act.copy(ab_t[:, 0:HALF], banks[2][0:2 * LR, :]).then_inc(ab_done, 1)
        act.copy(ab_t[:, HALF:S], banks[3][0:2 * LR, :]).then_inc(ab_done, 1)
        leave_phase(act)
        enter_phase(act, 1)

        def act_weights(h):
            for g in range(NG):
                act.wait_ge(c_diff, 3 * h + g + 1)
                act.activation(e8[:, g, :], e8[:, g, :], ACT.Exp, scale=SCALE).then_inc(c_exp, 1)

        def act_head_a(h, behind):
            for s in range(2 * TA):
                k, xh = s // 2, s % 2
                if xh == 0:
                    act.wait_ge(st_ready, 2 * TA * h + 2 * k)
                    hi_tile(k + 2, 3 * h + (k + 2) // 3 + 1)
                act.wait_ge(st_ready, 2 * TA * h + s + 1)
                if k == 0:
                    act.wait_ge(vtr_ready, 6 * h)
                    dst = v_raw[:, HALF * xh:HALF * xh + HALF]
                elif k <= 4:
                    j = s - 2
                    act.wait_ge(t1_ready, 8 * h + (j - 1 if j >= 2 else 0))
                    dst = qk_raw[:, xh, :]
                else:
                    act.wait_ge(gate_out[xh], 16 * (4 * h + k - 5))
                    dst = gbuf[:, xh, :]
                act.copy(dst, banks[xh]).then_inc(st_evac, 1)
                if k > 4:
                    act.wait_ge(st_evac, 2 * TA * h + s + 1)
                    act.dma_start(gate_d[bass.ds(4 * h + k - 5, 1)].rearrange("a p t -> (a p) t")
                                  [:, HALF * xh:HALF * xh + HALF], gbuf[:, xh, :]).then_inc(gate_out[xh], 16)
                for job in JOBS_A.get(s, []):
                    j = int(job[1:])
                    if job[0] == "v":
                        act.wait_ge(vtr_ready, 6 * h + j + 1)
                        act.wait_ge(pv_ready, NB * h)
                        act.copy(vt[:, 4 * j:4 * j + 4, :],
                                 x_ps[X_ORDER.index(job) % 2].rearrange("p (u d) -> p u d", d=P)
                                 ).then_inc(v_evac, 1)
                    elif job[0] == "a":
                        act.wait_ge(t1_ready, 8 * h + j + 1)
                        act.wait_ge(rot_done, 16 * h + 2 * j)
                        act.activation(rc[:, :, :],
                                       x_ps[X_ORDER.index(job) % 2].rearrange("p (t d) -> p t d", d=P),
                                       ACT.Square).then_inc(t1_sq, 1)
                    elif job[0] == "b":
                        act.wait_ge(t2_ready, 8 * h + j + 1)
                        act.wait_ge(s_ready, NB * h)
                        act.copy(qk_t[:, j // 2, HALF * (j % 2):HALF * (j % 2) + HALF],
                                 x_ps[X_ORDER.index(job) % 2]).then_inc(t2_evac, 1)
                    else:
                        if 2 <= j < NB + 2:
                            b = j - 2
                            act.wait_ge(pt_ready, NB * h + b + 1)
                            act.wait_ge(pv_ready, NB * h + (b - 1 if b >= 2 else 0))
                            if b >= 8:
                                o, i_ = pt[:, b % 2, :, 1, :], pt_ps.rearrange(
                                    "p (i k q) -> p i k q", i=2, k=2)[:, :, 1, :]
                            else:
                                lo = P if (b == 0 or b >= 4) else 0
                                o = pt[:, b % 2, :, :, :].rearrange("p i k q -> p (i k q)")[:, lo:]
                                i_ = pt_ps[:, lo:]
                            act.copy(o, i_).then_inc(pt_evac, 1)
                        if j < NB:
                            act.wait_ge(neg_max, NB * h + j + 1)
                            for i in range(2):
                                g, _, prev = unit(j, i)
                                lo = 0 if prev else P
                                u = 2 * j + i
                                t = sm[:, j % 3, i, lo:]
                                act.activation(t, t, ACT.Exp, bias=nmax[:, u:u + 1], scale=SCALE,
                                               accum_out=stats[:, NU + u:NU + u + 1]).then_inc(p_done, 1)
                if behind and s == 2:
                    act_weights(h - 1)
            act.wait_ge(stat_tr, h + 1)
            act.wait_ge(stat_out, 16 * h)
            act.copy(stat_sb[:, :], pt_ps[0:2 * NU, 0:P]).then_inc(stat_sbd, 1)

        act_head_a(0, False)
        with act.Fori(1, H) as h:
            act_head_a(h, True)
        act.wait_ge(gate_out[0], 16 * 2 * NK)
        act.wait_ge(gate_out[1], 16 * 2 * NK)
        leave_phase(act)
        enter_phase(act, 2)

        def act_head(h, tail):
            base = 2 * B0 + 2 * TB * h
            act.wait_ge(z_ready, 2 * h)
            act.wait_ge(z_min, 2 * h)
            act.copy(w_up_h[:, :], w_up[:, bass.ds(P * h, P)]).then_inc(up_copied, 1)
            act.copy(b_a_h[:, :], b_a[:, bass.ds(h, 1)]).then_inc(up_copied, 1)

            def act_z(xh):
                n = 2 * h + xh
                act.wait_ge(z_ready, n + 1)
                act.wait_ge(b_done, 8 * h + 4 * xh)
                act.wait_ge(up_copied, 2 * h + 2)
                act.activation(za[:, :], o_ps, ACT.Abs, bias=b_a_h[:, 0:1]).then_inc(z_abs, 1)
                act.wait_ge(z_abs, n + 1)
                act.activation(za[:, :], za[:, :], ACT.Exp, scale=-1.0).then_inc(z_ln, 1)
                act.wait_ge(z_ln, 2 * n + 1)
                act.activation(za[:, :], za[:, :], ACT.Ln, bias=1.0).then_inc(z_ln, 1)

            def act_e(p):
                for lv in range(8):
                    act.wait_ge(d_done, 64 * h + 16 * p + 2 * lv + 2)
                    t = dbuf[:, lv, :]
                    act.activation(t, t, ACT.Exp, scale=1.0 / TEMP).then_inc(e_done, 1)
                t = qh[:, 2 * P * p:2 * P * p + 2 * P]
                if tail:
                    act.wait_ge(kv_ready, 8 * (h - 1) + 2 * p + 2)
                act.activation(t, bcum[:, 2 * P * p:2 * P * p + 2 * P], ACT.Exp,
                               scale=1.0 / TEMP).then_inc(e_done, 1)
                if tail:
                    act.wait_ge(state_done, 8 * (h - 1) + 2 * p + 2)
                act.activation(elast[:, 2 * p:2 * p + 2], bcum[:, 2 * P * p + P - 1:2 * P * p + 2 * P:P],
                               ACT.Exp, scale=1.0 / TEMP).then_inc(el_done, 1)

            for s in range(2 * TB):
                k, xh = s // 2, s % 2
                if xh == 0:
                    act.wait_ge(st_ready, base + 2 * k)
                    hi_tile(k + 2, B0 // 3 + 2 * h + (k + 2) // 3 + 1)
                act.wait_ge(st_ready, base + s + 1)
                if k == 0:
                    act.wait_ge(l_ready, 8 * h)
                    act.copy(kf[:, HALF * xh:HALF * xh + HALF], banks[xh]).then_inc(st_evac, 1)
                elif k == 1:
                    act.mul(qf[:, HALF * xh:HALF * xh + HALF], banks[xh], SCALE).then_inc(st_evac, 1)
                else:
                    if not tail and s == 8:
                        act.wait_ge(oa_out, 16 * H)
                    if s < 8:
                        act.wait_ge(vb_ready, 4 * h + (s - 5 if s >= 6 else 0))
                        act.copy(raw2[:, xh, :], banks[xh]).then_inc(st_evac, 1)
                    else:
                        act.wait_ge(ob_gated, 4 * h)
                        act.copy(g_t[:, (s - 8) // 2, HALF * xh:HALF * xh + HALF], banks[xh]).then_inc(st_evac, 1)
                for kind, j, jh in jobs_b(s, h, tail):
                    if kind == "z":
                        act_z(j)
                    elif kind == "v":
                        e, vh = j // 2, j % 2
                        act.wait_ge(vb_ready, 4 * h + j + 1)
                        act.wait_ge(kv_ready, 8 * h)
                        if not tail and j == 0:
                            act.wait_ge(wgt_out, 16 * H)
                        act.copy(vtok[:, 4 * vh:4 * vh + 4, P * e:P * e + P],
                                 bank3.rearrange("p (c d) -> p c d", d=P)).then_inc(vb_evac, 1)
                    elif kind == "l":
                        act.wait_ge(kh_ready, 8 * h + j + 1)
                        act.wait_ge(kv_ready, 8 * h)
                        act.copy(khat[:, j, :], s_ps[:, P * (j % 4):P * (j % 4) + P]).then_inc(kh_evac, 1)
                    else:
                        (act_m if kind == "m" else act_t)(jh, j)
                if s in E_AFTER:
                    act_e(E_AFTER[s])
                if tail and s == 2:
                    act_silu(h - 1)
                if not tail and s == 1:
                    act_weights(H - 1)

        E_AFTER = {2: 0, 3: 1, 5: 2, 6: 3}

        def act_silu(h):
            act.wait_ge(st_evac, 2 * B0 + 2 * TB * (h + 1))
            act.activation(g_t[:, :, :], g_t[:, :, :], ACT.Silu).then_inc(g_done, 1)
            act.preload_act_table_set("natural_log_exp_and_others")

        def act_square(h, j, ps):
            n = 8 * h + j
            act.wait_ge(kv_ready, n + 1)
            act.wait_ge(o_sq, n)
            act.activation(osq[:, :], ps[:, 0:DV], ACT.Square,
                           accum_out=ost[:, 0, j:j + 1]).then_inc(o_sq, 1)

        def act_normed(h, j, ps):
            act.wait_ge(o_rstd, 8 * h + j + 1)
            act.wait_ge(obt_ready, 8 * h + (j - 1 if j >= 2 else 0))
            act.activation(obn[:, j % 2, :], ps[:, 0:DV], ACT.Copy,
                           scale=ost[:, 2, j:j + 1]).then_inc(obn_done, 1)

        def act_m(h, j):
            act_square(h, j, ok_ps)
            act_normed(h, j, ok_ps)

        def act_t(h, j):
            act.wait_ge(obt_ready, 8 * h + j + 1)
            act.wait_ge(ob_out, 16 * h)
            act.copy(ob_t[:, :, P * j:P * j + P],
                     bank3[:, 0:2 * P].rearrange("p (e t) -> p e t", e=2)).then_inc(obt_evac, 1)

        act_head(0, False)
        with act.Fori(1, H) as h:
            act_head(h, True)

        def split_hi(i):
            if i == 0:
                act.wait_ge(kh_ready, 8 * H)
                act.wait_ge(att_done, 8 * H)
            if i == H:
                act.wait_ge(st_ready, 2 * B0 + 2 * TB * H)
            if i < N_ST:
                act.wait_ge(stage_in[i % 4], 16 * (i // 4 + 1))
                src = stage[:, i % 4, :]
            else:
                act.wait_ge(ob_gated, 4 * (H - 1) + 2 * (i - N_ST) + 2)
                src = ob_t[:, i - N_ST, :]
            dst = oa_hi[:, i, :] if i < H else act_hi[:, i - H, :]
            act.copy(dst, src).then_inc(stage_hi, 1)

        def sigmoids(i, f):
            for xh in range(2):
                act.wait_ge(gl_in[xh], 16 * (2 * i + f + 1))
                act.activation(gl[:, xh, :, :], gl[:, xh, :, :], ACT.Sigmoid).then_inc(sig_done, 1)

        for c in range(4, 8):
            act_square(H - 1, c, rest_ps(c))
            if c < 7:
                split_hi(2 * (c - 4))
            act_normed(H - 1, c, rest_ps(c))
            act_t(H - 1, c - 1)
            if c < 7:
                split_hi(2 * (c - 4) + 1)
        split_hi(6)
        split_hi(7)
        act_silu(H - 1)
        act_t(H - 1, 7)
        for i in range(8, H + 2 * H):
            split_hi(i)
        hi_tile(2, C0 // 3 + 1)
        sigmoids(0, 0)
        leave_phase(act)
        enter_phase(act, 3)

        def pair_loop(i, it0, turn0, fn, start=False, end=False):
            for k in range(TC):
                if k == 0:
                    act.wait_ge(down_ready, 16 * (it0 + i))
                elif k < 5:
                    act.wait_ge(mix_ready, 8 * (it0 + i) + 2 * k)
                else:
                    act.wait_ge(down_ready, 16 * (it0 + i) + 16)
                if not (end and k >= 4) and not (start and k == 0):
                    hi_tile(k + 2, turn0 + 2 * i + (k + 2) // 3 + 1)
                fn(k)

        def hi_y(it, w):
            f, xh = w // 2, w % 2
            act.wait_ge(y_done, 4 * it + w + 1)
            act.wait_ge(down_ready, 16 * it)
            act.copy(y_hi[:, f, HALF * xh:HALF * xh + HALF], yf[:, xh, :]).then_inc(yhi_done, 1)

        def merge_pair(i, start, end):
            def merge(k):
                if k == 2 or (k == 0 and not start):
                    sigmoids(i, k // 2)
                if k in (1, 3):
                    hi_y(i, k - 1)
                    hi_y(i, k)
                if k == 4 and end:
                    for tt in range(NT):
                        act.wait_ge(acc_done, 16 * (NC_IT - 1) + 2 * tt + 2)
                        act.activation(xn[:, tt, :], xk[:, tt, :], ACT.Square,
                                       accum_out=ssq[:, tt:tt + 1]).then_inc(ssq_done, 1)
            pair_loop(i, 0, C0 // 3, merge, start=start)

        merge_pair(0, True, False)
        with act.Fori(1, NC_IT - 1) as i:
            merge_pair(i, False, False)
        merge_pair(NC_IT - 1, False, True)
        norm_hi(1, gain2)

        def ffn(i, last):
            it = NC_IT + i

            def silu(k):
                if k in (0, 2):
                    for xh in range(2):
                        w = k + xh
                        act.wait_ge(mix_ready, 8 * it + 4 * (k // 2) + xh + 1)
                        act.wait_ge(y_done, 4 * it + (w - 1 if w >= 2 else 0))
                        act.activation(gl[:, xh, 0, :], banks[xh], ACT.Silu).then_inc(sig_done, 1)
                if k in (1, 3):
                    hi_y(it, k - 1)
                    hi_y(it, k)
            pair_loop(i, NC_IT, D0 // 3, silu, end=last)

        with act.Fori(0, ND_IT - 1) as i:
            ffn(i, False)
        ffn(ND_IT - 1, True)

    @block.vector
    def _(dve):
        def lo_tile(n, k, width=1024):
            dve.wait_ge(hi_done, n + 1)
            dve.tensor_tensor(w_lo[:, slot_of(k), 0:width], w_raw[:, slot_of(k), 0:width],
                              w_hi[:, slot_of(k), 0:width].bitcast(F32), ALU.subtract).then_inc(lo_done, 1)

        def variance(j, size, i):
            cols = slice(size * i, size * i + size)
            dve.wait_ge(ssq_done, NT * j + size * i + size)
            dve.tensor_scalar(var[:, cols], ssq[:, cols], 1.0 / D, EPS, ALU.mult, ALU.add).then_inc(var_done, size)

        def normed(j, size, tt):
            xt, xo = (xk, xn) if j else (xin, xin)
            dve.wait_ge(rstd_done, NT * j + size * (tt // size) + size)
            dve.tensor_scalar(xo[:, tt, :], xt[:, tt, :], rstd[:, tt:tt + 1], None, ALU.mult).then_inc(xn_done, 1)

        def norm_lo(j, g, gain):
            xh, kt = g // NK, g % NK
            dve.wait_ge(nt_hi, 16 * j + g + 1)
            hs = act_hi[:, kt, HALF * xh:HALF * xh + HALF].bitcast(F32)
            dve.scalar_tensor_tensor(out=act_lo[:, kt, HALF * xh:HALF * xh + HALF], in0=banks[g % 8],
                                     scalar=gain[:, kt:kt + 1], in1=hs, op0=ALU.mult,
                                     op1=ALU.subtract).then_inc(nt_lo, 1)

        for tt in range(4):
            variance(0, 1, tt)
            normed(0, 1, tt)
        for g in range(2 * NK):
            if g % 2 == 0 and g < NK:
                variance(0, 1, 4 + g // 2)
                normed(0, 1, 4 + g // 2)
            if g == 6:
                dve.wait_ge(ab_hi_done, 1)
                dve.tensor_tensor(ab_w[:, :, LR:2 * LR], ab_raw[:, :, :], ab_w[:, :, 0:LR].bitcast(F32),
                                  ALU.subtract).then_inc(ab_lo_done, 1)
            norm_lo(0, g, gain1)
        lo_tile(0, 0)
        lo_tile(1, 1)
        dve.wait_ge(pos_in, 16 * 2)
        steps = [0]

        def step(ins):
            steps[0] += 1
            ins.then_inc(pos_step, 1)
            dve.wait_ge(pos_step, steps[0])

        step(dve.tensor_copy(posf[:, :], posi[:, :]))
        step(dve.tensor_tensor(ang[:, :, :], posf[:, :, None].broadcast_to([P, NT, 64]),
                               invf[:, None, :].broadcast_to([P, NT, 64]), ALU.mult))
        for shift, t in ((0.0, tra), (0.25, trb)):
            tt_ = t[:, :, :]
            step(dve.tensor_scalar(tt_, ang[:, :, :], 1.0 / TWO_PI, shift, ALU.mult, ALU.add))
            step(dve.tensor_scalar(tt_, tt_, ROUND, -ROUND, ALU.add, ALU.add))
            r1 = red[:, :, :]
            step(dve.scalar_tensor_tensor(out=r1, in0=tt_, scalar=-PI_C1, in1=ang[:, :, :],
                                          op0=ALU.mult, op1=ALU.add))
            step(dve.scalar_tensor_tensor(out=r1, in0=tt_, scalar=-PI_C2, in1=r1, op0=ALU.mult, op1=ALU.add))
            step(dve.scalar_tensor_tensor(out=r1, in0=tt_, scalar=-PI_C3, in1=r1, op0=ALU.mult, op1=ALU.add))
            step(dve.tensor_scalar(tt_, r1, shift * TWO_PI, PI_SAFE, ALU.add, ALU.min))
            step(dve.tensor_scalar(tt_, tt_, -PI_SAFE, None, ALU.max))
        dve.wait_ge(pool_const, 5)
        dve.tensor_scalar(parj[:, :], pari[:, :], 1, None, ALU.bitwise_and).then_inc(par_done, 1)
        dve.wait_ge(par_done, 1)
        dve.tensor_scalar(parf[:, :], parj[:, :], NEG, None, ALU.mult).then_inc(par_done, 1)
        leave_phase(dve)
        enter_phase(dve, 1)


        def order(t, g):
            if g == 1:
                return t.rearrange("c (r jl) -> c jl r", r=4)
            if g == 2:
                return t.rearrange("c (r il) -> c il r", r=8)
            return t

        def like(t, g):
            if g == 1:
                return t.rearrange("c (jl r) -> c jl r", r=4)
            if g == 2:
                return t.rearrange("c (il r) -> c il r", r=8)
            return t

        def merge_step(ins, n):
            ins.then_inc(c_step, 1)
            dve.wait_ge(c_step, n)

        def merge_diffs(h):
            dve.wait_ge(stat_in, 16 * 8 * (h + 1))
            merge_step(dve.tensor_copy(mm8[:, :], st8[:, 0, 0, :]), 8 * h + 1)
            for g in (1, 2):
                merge_step(dve.tensor_tensor(like(mm8[:, :], g), order(st8[:, 0, g, :], g), like(mm8[:, :], g),
                                             ALU.max), 8 * h + 1 + g)
            dve.wait_ge(wgt_out, 16 * h)
            for g in range(NG):
                dve.tensor_tensor(like(e8[:, g, :], g), order(st8[:, 0, g, :], g), like(mm8[:, :], g),
                                  ALU.subtract).then_inc(c_diff, 1)

        def merge_norm(h):
            for g in range(NG):
                dve.wait_ge(c_exp, 3 * h + g + 1)
                merge_step(dve.tensor_tensor(like(z8[:, g, :], g), order(st8[:, 1, g, :], g), like(e8[:, g, :], g),
                                             ALU.mult), 8 * h + 4 + g)
            merge_step(dve.tensor_reduce(z8[:, NG, :], z8[:, 0:NG, :].rearrange("c g t -> c t g"), AX.X, ALU.add),
                       8 * h + 7)
            merge_step(dve.reciprocal(z8[:, NG, :], z8[:, NG, :]), 8 * h + 8)
            for g in range(NG):
                dve.tensor_tensor(e8[:, g, :], e8[:, g, :], z8[:, NG, :], ALU.mult).then_inc(c_wgt, 1)

        def merge_mul(h, g):
            dve.wait_ge(wb_in, 16 * h + 16)
            dve.wait_ge(u_done, NB * h + NB)
            ut = u_t[:, 8 * g:8 * g + 8, :]
            if g == 0:
                w_, u_ = wb[:, 0, :].rearrange("p (u q) -> p u q", u=8), ut
            elif g == 1:
                w_ = wb[:, 1, :].rearrange("p (b j r) -> p b j r", b=2, r=4)
                u_ = ut.rearrange("p (r b) j -> p b j r", b=2)
            else:
                w_ = wb[:, 2, :].rearrange("p (i r) -> p i r", r=8)
                u_ = ut.rearrange("p r i -> p i r")
            dve.tensor_tensor(w_, w_, u_, ALU.mult).then_inc(wb_mul, 1)

        def dve_head_a(h, behind):
            for s in range(2 * TA):
                k, xh = s // 2, s % 2
                if xh == 0:
                    lo_tile(TA * h + k + 2, k + 2)
                for job in JOBS_A.get(s, []):
                    j = int(job[1:])
                    if job[0] == "a":
                        n = 8 * h + j
                        ps = x_ps[X_ORDER.index(job) % 2].rearrange("p (t d) -> p t d", d=P)
                        dve.wait_ge(t1_sq, n + 1)
                        dve.tensor_reduce(qk_st[:, 0, j, :], rc[:, :, :], AX.X, ALU.add).then_inc(t1_ss, 1)
                        dve.wait_ge(t1_ss, n + 1)
                        dve.tensor_scalar(qk_st[:, 1, j, :], qk_st[:, 0, j, :], 1.0 / P, EPS,
                                          ALU.mult, ALU.add).then_inc(t1_var, 1)
                        dve.wait_ge(t1_rstd, n + 1)
                        dve.wait_ge(t1_sin, n)
                        gain = k_gain if j < 2 else q_gain
                        for i in range(4):
                            dve.scalar_tensor_tensor(out=qg[:, i, :], in0=ps[:, i, :], scalar=qk_st[:, 2, j, i:i + 1],
                                                     in1=gain[:, :], op0=ALU.mult, op1=ALU.mult).then_inc(t1_gain, 1)
                        dve.wait_ge(t1_gain, 4 * n + 4)
                        dve.wait_ge(rot_done, 2 * n)
                        cb = cos_t[:, 4 * (j % 2):4 * (j % 2) + 4, None, :].broadcast_to([P, 4, 2, 64])
                        dve.tensor_tensor(rc[:, :, :].rearrange("p t (a f) -> p t a f", a=2),
                                          qg[:, :, :].rearrange("p t (a f) -> p t a f", a=2), cb,
                                          ALU.mult).then_inc(t1_cos, 1)
                        dve.tensor_tensor(rs[:, :, 64:128], qg[:, :, 0:64], sin_t[:, 4 * (j % 2):4 * (j % 2) + 4, :],
                                          ALU.mult).then_inc(t1_cos, 1)
                        dve.wait_ge(t1_cos, 2 * n + 2)
                        dve.wait_ge(t1_sin, n + 1)
                        dve.wait_ge(t2_ready, 8 * h + (j - 1 if j >= 2 else 0))
                        dve.tensor_tensor(rot[:, j % 2, :, 0:64], rc[:, :, 0:64], rs[:, :, 0:64],
                                          ALU.subtract).then_inc(rot_done, 1)
                        dve.tensor_tensor(rot[:, j % 2, :, 64:128], rc[:, :, 64:128], rs[:, :, 64:128],
                                          ALU.add).then_inc(rot_done, 1)
                    elif job[0] == "s":
                        if j < NB:
                            dve.wait_ge(s_ready, NB * h + j + 1)
                            dve.wait_ge(pt_ready, NB * h + (j - 2 if j >= 3 else 0))
                            dve.wait_ge(stat_tr, h)
                            alone(dve)
                            for i in range(2):
                                g, _, prev = unit(j, i)
                                lo = 0 if prev else P
                                mask = wide[:, :] if g == 2 else near[:, lo:]
                                u = 2 * j + i
                                dve.tensor_tensor_reduce(sm[:, j % 3, i, lo:], score_ps[j % 2][:, 2 * P * i + lo:2 * P * i + 2 * P],
                                                         mask, 1.0, -3.0e38, ALU.add, ALU.max,
                                                         stats[:, u:u + 1]).then_inc(masked, 1)
                            dve.wait_ge(masked, NU * h + 2 * j + 2)
                            dve.tensor_scalar(nmax[:, 2 * j:2 * j + 2], stats[:, 2 * j:2 * j + 2], -SCALE, None,
                                              ALU.mult).then_inc(neg_max, 1)
                        if j >= 3:
                            b = j - 3
                            dve.wait_ge(pv_ready, NB * h + b + 1)
                            dve.wait_ge(wb_mul, 3 * h)
                            dve.tensor_copy(u_t[:, 2 * b:2 * b + 2, :],
                                            o_ps[:, 2 * P * (b % 2):2 * P * (b % 2) + 2 * P]
                                            .rearrange("p (u q) -> p u q", u=2)).then_inc(u_done, 1)
                if behind and s == 1:
                    merge_diffs(h - 1)
                if behind and s == 2:
                    merge_norm(h - 1)
                if behind and 5 <= s <= 7:
                    merge_mul(h - 1, s - 5)

        dve_head_a(0, False)
        with dve.Fori(1, H) as h:
            dve_head_a(h, True)
        leave_phase(dve)
        enter_phase(dve, 2)

        def dve_head(h, tail):
            def dve_z(xh):
                n = 2 * h + xh
                dve.wait_ge(z_abs, n + 1)
                dve.wait_ge(b_done, 8 * h + 4 * xh)
                dve.wait_ge(up_copied, 2 * h + 2)
                dve.tensor_scalar(zm[:, :], o_ps, b_a_h[:, 0:1], 0.0, ALU.add, ALU.min).then_inc(z_min, 1)
                dve.wait_ge(z_min, n + 1)
                dve.wait_ge(z_ln, 2 * n + 2)
                if xh == 0:
                    dve.wait_ge(el_done, 4 * h)
                    dve.wait_ge(d_done, 64 * h)
                for c in range(4):
                    cols = slice(HALF * xh + P * c, HALF * xh + P * c + P)
                    dve.tensor_tensor_scan(bcum[:, cols], zm[:, P * c:P * c + P], za[:, P * c:P * c + P], 0.0,
                                           ALU.add, ALU.subtract).then_inc(b_done, 1)

            def dve_f(p):
                cols = slice(2 * P * p, 2 * P * p + 2 * P)
                if p == 0:
                    dve.wait_ge(st_evac, 2 * B0 + 2 * TB * h + 3)
                if p == 2:
                    dve.wait_ge(st_evac, 2 * B0 + 2 * TB * h + 4)
                dve.wait_ge(kh_ready, 8 * h + (2 * (p - 1) if p >= 2 else 0))
                for lv in range(7):
                    m = 64 >> lv
                    dve.wait_ge(e_done, 36 * h + 9 * p + lv + 1)
                    fv, ev, kv, qv = (t.rearrange("p (n two m) -> p n two m", two=2, m=m) for t in
                                      (fbuf[:, p % 2, lv, :], dbuf[:, lv, :], kf[:, cols], qf[:, cols]))
                    dve.tensor_tensor(fv[:, :, 0, :], kv[:, :, 0, :], ev[:, :, 0, :], ALU.mult)
                    dve.tensor_tensor(fv[:, :, 1, :], qv[:, :, 1, :], ev[:, :, 1, :], ALU.mult).then_inc(f_done, 1)
                dve.wait_ge(e_done, 36 * h + 9 * p + 8)
                dve.tensor_tensor(fbuf[:, p % 2, 7, :], kf[:, cols], dbuf[:, 7, :], ALU.mult).then_inc(f_done, 1)
                dve.wait_ge(e_done, 36 * h + 9 * p + 9)
                t = qh[:, cols]
                dve.tensor_tensor(t, qf[:, cols], t, ALU.mult).then_inc(f_done, 1)

            def dve_l(c):
                n = 8 * h + c
                dve.wait_ge(l_ready, n + 1)
                dve.wait_ge(att_done, n)
                for b in range(2):
                    dve.tensor_tensor(lvm[:, 4 * b:4 * b + 4, :],
                                      lvl_ps[:, b, :].rearrange("p (l t) -> p l t", t=P),
                                      gmask[:, 4 * b:4 * b + 4, :], ALU.mult).then_inc(l_mask, 1)
                dve.wait_ge(l_mask, 2 * n + 2)
                if c == 0:
                    dve.wait_ge(kv_ready, 8 * h)
                dve.tensor_reduce(att[:, c, :], lvm[:, :, :].rearrange("p l t -> p t l"), AX.X,
                                  ALU.add).then_inc(att_done, 1)

            for s in range(2 * TB):
                k, xh = s // 2, s % 2
                if xh == 0:
                    lo_tile(B0 + TB * h + k + 2, k + 2)
                for kind, j, jh in jobs_b(s, h, tail):
                    if kind == "z":
                        dve_z(j)
                    elif kind == "l":
                        if not tail and j == 0:
                            dve.wait_ge(pool_const, 8 + 24)
                        dve_l(j)
                    elif kind == "m":
                        dve_m(jh, j, ok_ps)
                if s in F_AFTER:
                    dve_f(F_AFTER[s])
                if tail and s == 4:
                    dve_gate(h - 1)
                if not tail and s == 0:
                    merge_diffs(H - 1)
                if not tail and s == 1:
                    merge_norm(H - 1)
                if not tail and s == 3:
                    merge_mul(H - 1, 0)
                if not tail and s == 4:
                    merge_mul(H - 1, 1)
                    merge_mul(H - 1, 2)

        F_AFTER = {2: 0, 3: 1, 5: 2, 7: 3}

        def dve_m(h, c, ps):
            n = 8 * h + c
            dve.wait_ge(o_sq, n + 1)
            if c == 0:
                dve.tensor_copy(state[:, 1, :], ps[:, DV:2 * DV]).then_inc(state_done, 1)
            else:
                dve.wait_ge(state_done, n)
                dve.wait_ge(el_done, 4 * h + c // 2 + 1)
                dve.scalar_tensor_tensor(out=state[:, (c + 1) % 2, :], in0=state[:, c % 2, :],
                                         scalar=elast[:, c:c + 1], in1=ps[:, DV:2 * DV],
                                         op0=ALU.mult, op1=ALU.add).then_inc(state_done, 1)
            dve.tensor_scalar(ost[:, 1, c:c + 1], ost[:, 0, c:c + 1], 1.0 / DV, EPS,
                              ALU.mult, ALU.add).then_inc(o_var, 1)

        def dve_gate(h):
            dve.wait_ge(g_done, h + 1)
            for j in range(4):
                e, xh = j // 2, j % 2
                dve.wait_ge(obt_evac, 8 * h + 4 * xh + 4)
                t = ob_t[:, e, HALF * xh:HALF * xh + HALF]
                dve.scalar_tensor_tensor(out=t, in0=t, scalar=gn[:, e:e + 1],
                                         in1=g_t[:, e, HALF * xh:HALF * xh + HALF], op0=ALU.mult,
                                         op1=ALU.mult).then_inc(ob_gated, 1)

        dve_head(0, False)
        with dve.Fori(1, H) as h:
            dve_head(h, True)

        def split_lo(i):
            dve.wait_ge(stage_hi, i + 1)
            src = stage[:, i % 4, :] if i < N_ST else ob_t[:, i - N_ST, :]
            hi, lo = (oa_hi[:, i, :], oa_lo[:, i, :]) if i < H else (act_hi[:, i - H, :], act_lo[:, i - H, :])
            dve.tensor_tensor(lo, src, hi.bitcast(F32), ALU.subtract).then_inc(stage_lo, 1)

        for c in range(4, 8):
            dve_m(H - 1, c, rest_ps(c))
            if c > 4:
                split_lo(2 * (c - 5))
                split_lo(2 * (c - 5) + 1)
        split_lo(6)
        split_lo(7)
        dve_gate(H - 1)
        for i in range(8, H + 2 * H):
            split_lo(i)
        lo_tile(C0 + 2, 2)
        leave_phase(dve)
        enter_phase(dve, 3)

        def finish_pair(it, n0, last, make_y, start=False, beside=None):
            for k in range(TC):
                if k == 5 and beside:
                    beside(16)
                if k != 4 and not (last and k == 5) and not (start and k == 0):
                    lo_tile(n0 + k + 2, k + 2)
                if k in (1, 3):
                    for w in (k - 1, k):
                        make_y(w)
                        f, xh = w // 2, w % 2
                        dve.wait_ge(yhi_done, 4 * it + w + 1)
                        dve.tensor_tensor(y_lo[:, f, HALF * xh:HALF * xh + HALF], yf[:, xh, :],
                                          y_hi[:, f, HALF * xh:HALF * xh + HALF].bitcast(F32),
                                          ALU.subtract).then_inc(ylo_done, 1)
                if k == 4:
                    for d in range(16):
                        if d == 4 and not last:
                            lo_tile(n0 + k + 2, k + 2)
                        if beside:
                            beside(d)
                        tt, nh = d // 2, d % 2
                        dve.wait_ge(down_ready, 16 * it + d + 1)
                        t = xk[:, tt, HALF * nh:HALF * nh + HALF]
                        if d == 0:
                            dve.wait_ge(acc_done, 16 * it)
                        if start and d % 8 == 0:
                            dve.wait_ge(xk_in[d // 8], 16 * NT // 2)
                        dve.tensor_tensor(t, banks[4 + d % 4], t, ALU.add).then_inc(acc_done, 1)

        def merge_pair(i, start=False, beside=None):
            def merge(w):
                f, xh = w // 2, w % 2
                dve.wait_ge(mix_ready, 8 * i + 4 * f + xh + 3)
                dve.wait_ge(sig_done, 4 * i + w + 1)
                dve.wait_ge(y_done, 4 * i + w)
                dve.wait_ge(yhi_done, 4 * i + (w - 1 if w >= 2 else 0))
                dve.wait_ge(ylo_done, 4 * i + (w - 1 if w >= 2 else 0))
                dve.tensor_tensor(ya[:, :], banks[xh], gl[:, xh, 0, :], ALU.mult).then_inc(mix_step, 1)
                dve.tensor_tensor(yb[:, :], banks[2 + xh], gl[:, xh, 1, :], ALU.mult).then_inc(mix_step, 1)
                dve.wait_ge(mix_step, 8 * i + 2 * w + 2)
                dve.tensor_tensor(yf[:, xh, :], ya[:, :], yb[:, :], ALU.add).then_inc(y_done, 1)

            finish_pair(i, C0 + TC * i, False, merge, start, beside)
        def norm2_first(d):
            if d == 10:
                variance(1, 4, 0)
            if 12 <= d < 16:
                normed(1, 4, d - 12)
            if d == 16:
                variance(1, 4, 1)

        merge_pair(0, start=True)
        with dve.Fori(1, NC_IT - 1) as i:
            merge_pair(i)
        merge_pair(NC_IT - 1, beside=norm2_first)
        for tt in range(4, NT):
            normed(1, 4, tt)
        for g in range(2 * NK):
            norm_lo(1, g, gain2)

        def ffn(i, last):
            it = NC_IT + i

            def swiglu(w):
                f, xh = w // 2, w % 2
                dve.wait_ge(mix_ready, 8 * it + 4 * f + xh + 3)
                dve.wait_ge(sig_done, 4 * it + w + 1)
                dve.wait_ge(yhi_done, 4 * it + (w - 1 if w >= 2 else 0))
                dve.wait_ge(ylo_done, 4 * it + (w - 1 if w >= 2 else 0))
                dve.tensor_tensor(yf[:, xh, :], banks[2 + xh], gl[:, xh, 0, :], ALU.mult).then_inc(y_done, 1)
            finish_pair(it, D0 + TC * i, last, swiglu)

        with dve.Fori(0, ND_IT - 1) as i:
            ffn(i, False)
        ffn(ND_IT - 1, True)

    @block.tensor
    def _(pe):
        def three(ps, lhs_hi, lhs_lo, rhs_hi, rhs_lo, first, last):
            pe.matmul(ps, lhs_hi, rhs_hi, start=first, stop=False)
            pe.matmul(ps, lhs_hi, rhs_lo, start=False, stop=False)
            return pe.matmul(ps, lhs_lo, rhs_hi, start=False, stop=last)

        def stream(ps, k, hi, lo, xh, kts=NK, staged=0):
            for kt in range(kts):
                if staged:
                    pe.wait_ge(stage_lo, staged + kt + 1)
                cols = slice(P * kt, P * kt + P)
                t = slice(HALF * xh, HALF * xh + HALF)
                mm = three(ps, w_hi[:, slot_of(k), cols], w_lo[:, slot_of(k), cols],
                           hi[:, kt, t], lo[:, kt, t], kt == 0, kt == kts - 1)
            return mm

        def norm_turn(j, xt):
            for g in range(2 * NK):
                xh, kt = g // NK, g % NK
                pe.wait_ge(xn_done, 8 * j + 4 * xh + 4)
                if j and g == 0:
                    pe.wait_ge(y_done, 4 * NC_IT)
                if j and g == 4:
                    pe.wait_ge(acc_done, 16 * NC_IT)
                if g >= 8:
                    pe.wait_ge(nt_lo, 16 * j + g - 7)
                for i in range(4):
                    tt = 4 * xh + i
                    mm = pe.transpose(banks[g % 8][:, P * i:P * i + P],
                                      xt[:, tt, P * kt:P * kt + P], ident[:, :])
                mm.then_inc(nt_ready, 1)

        pe.wait_ge(pool_const, 2)
        norm_turn(0, xin)
        pe.wait_ge(ab_lo_done, 1)
        for xh in range(2):
            pe.wait_ge(nt_lo, 16 if xh else 11)
            t = slice(HALF * xh, HALF * xh + HALF)
            for kt in range(NK):
                pe.matmul(banks[2 + xh][0:2 * LR, :], ab_w[:, kt, :], act_hi[:, kt, t], start=(kt == 0), stop=False)
                mm = pe.matmul(banks[2 + xh][0:2 * LR, :], ab_w[:, kt, :], act_lo[:, kt, t], start=False,
                               stop=(kt == NK - 1))
            mm.then_inc(ab_ready, 1)
        leave_phase(pe)

        def pe_head_a(h, behind):
            def x_bank(job):
                at = X_ORDER.index(job)
                if at < 2:
                    pe.wait_ge(t2_evac, 8 * h)
                else:
                    kind, j = X_ORDER[at - 2][0], int(X_ORDER[at - 2][1:])
                    if kind == "v":
                        pe.wait_ge(v_evac, 6 * h + j + 1)
                    elif kind == "a":
                        pe.wait_ge(t1_gain, 4 * (8 * h + j) + 4)
                    else:
                        pe.wait_ge(t2_evac, 8 * h + j + 1)
                return x_ps[at % 2]

            def pe_s(b):
                if b == 0:
                    pe.wait_ge(neg_max, NB * h)
                    pe.wait_ge(ab_done, 2)
                else:
                    pe.wait_ge(neg_max, NB * h + b - 1)
                need = {0: 3, 2: 4, 4: 6, 8: 8}
                if b in need:
                    pe.wait_ge(t2_evac, 8 * h + need[b])
                for i in range(2):
                    g, n, prev = unit(b, i)
                    q = tokens(qk_t[:, 1 + g, :], g, n)
                    o = score_ps[b % 2][:, 2 * P * i:2 * P * i + 2 * P]
                    if g == 0:
                        kk = qk_t[:, 0, P * (n - prev):P * n + P]
                    elif g == 1:
                        r = n // 2
                        kk = qk_t[:, 0, r:r + (8 if prev else 4) * P - 3:4]
                    else:
                        kk = tokens(qk_t[:, 0, :], g, n)
                    mm = pe.matmul(o if prev else o[:, P:], q, kk, start=True, stop=True)
                mm.then_inc(s_ready, 1)

            def pe_t(b):
                pe.wait_ge(p_done, NU * h + 2 * b + 2)
                if b == 0:
                    pe.wait_ge(stat_sbd, h)
                pe.wait_ge(pt_evac, NB * h + b)
                for i in range(2):
                    _, _, prev = unit(b, i)
                    for kb in range(0 if prev else 1, 2):
                        at = P * (2 * i + kb)
                        mm = pe.transpose(pt_ps[:, at:at + P], sm[:, b % 3, i, P * kb:P * kb + P], ident[:, :])
                mm.then_inc(pt_ready, 1)

            def pe_pv(b):
                pe.wait_ge(pt_evac, NB * h + b + 1)
                if b == 0:
                    pe.wait_ge(v_evac, 6 * h + 6)
                pe.wait_ge(u_done, NB * h + b)
                for i in range(2):
                    g, n, prev = unit(b, i)
                    o = o_ps[:, P * (2 * (b % 2) + i):P * (2 * (b % 2) + i) + P]
                    u = 8 * g + n
                    if prev:
                        pe.matmul(o, vt[:, u - 1, :], pt[:, b % 2, i, 0, :], start=True, stop=False)
                    mm = pe.matmul(o, vt[:, u, :], pt[:, b % 2, i, 1, :], start=not prev, stop=True)
                mm.then_inc(pv_ready, 1)

            for s in range(2 * TA):
                k, xh = s // 2, s % 2
                if xh == 0:
                    pe.wait_ge(lo_done, TA * h + k + 1)
                if s or behind:
                    pe.wait_ge(st_evac, 2 * TA * h + s - 1)
                stream(banks[xh], k, act_hi, act_lo, xh).then_inc(st_ready, 1)
                for job in JOBS_A.get(s, []):
                    j = int(job[1:])
                    if job[0] == "v":
                        ps = x_bank(job)
                        pe.wait_ge(st_evac, 2 * TA * h + (1 if j == 0 else 2))
                        for i in range(4):
                            u = 4 * j + i
                            mm = pe.transpose(ps[:, P * i:P * i + P], tokens(v_raw[:, :], u // 8, u % 8), ident[:, :])
                        mm.then_inc(vtr_ready, 1)
                    elif job[0] == "a":
                        ps = x_bank(job)
                        pe.wait_ge(st_evac, 2 * TA * h + j + 3)
                        for i in range(4):
                            mm = pe.transpose(ps[:, P * i:P * i + P], qk_raw[:, j % 2, P * i:P * i + P], ident[:, :])
                        mm.then_inc(t1_ready, 1)
                    elif job[0] == "b":
                        ps = x_bank(job)
                        pe.wait_ge(rot_done, 16 * h + 2 * j + 2)
                        for i in range(4):
                            mm = pe.transpose(ps[:, P * i:P * i + P], rot[:, j % 2, i, :], ident[:, :])
                        mm.then_inc(t2_ready, 1)
                    else:
                        if j < NB:
                            pe_s(j)
                        if 2 <= j < NB + 2:
                            pe_t(j - 2)
                        if j >= 3:
                            pe_pv(j - 3)
            pe.wait_ge(p_done, NU * h + NU)
            pe.wait_ge(pt_evac, NB * h + NB)
            alone(pe)
            pe.transpose(pt_ps[0:2 * NU, 0:P], stats[:, :], ident[:, :]).then_inc(stat_tr, 1)
        pe_head_a(0, False)
        with pe.Fori(1, H) as h:
            pe_head_a(h, True)
        leave_phase(pe)

        def pe_head(h, tail):
            base = 2 * B0 + 2 * TB * h
            if not tail:
                after_a = {0: (u_done, NB * H), 4: (neg_max, NB * H), 5: (stat_sbd, H)}
            else:
                after_a = {}

            def pe_z(xh):
                n = 2 * h + xh
                if xh == 0:
                    pe.wait_ge(up_copied, 2 * h + 2)
                pe.wait_ge(z_abs, n)
                pe.wait_ge(z_min, n)
                pe.matmul(o_ps, w_up_h[:, :], ab_t[:, HALF * xh:HALF * xh + HALF], start=True,
                          stop=True).then_inc(z_ready, 1)

            def pe_v(j):
                pe.wait_ge(st_evac, base + 4 + j + 1)
                if j == 0:
                    pe.wait_ge(obt_evac, 8 * h)
                else:
                    pe.wait_ge(vb_evac, 4 * h + j)
                for i in range(4):
                    mm = pe.transpose(bank3[:, P * i:P * i + P], raw2[:, j % 2, P * i:P * i + P], ident[:, :])
                mm.then_inc(vb_ready, 1)

            def pe_l(c):
                p, cols = c // 2, slice(P * (c % 2), P * (c % 2) + P)
                n = 8 * h + c
                pe.wait_ge(f_done, 36 * h + 9 * p + 9)
                if c % 4 == 0:
                    pe.wait_ge(st_evac, base + 3 + c // 4)
                pe.wait_ge(l_mask, 2 * n)
                for lv in range(7):
                    t = fbuf[:, p % 2, lv, cols]
                    pe.matmul(lvl_ps[:, lv // 4, P * (lv % 4):P * (lv % 4) + P], t, t, start=True, stop=True)
                ct = slice(P * c, P * c + P)
                pe.matmul(lvl_ps[:, 1, 3 * P:4 * P], kf[:, ct], qf[:, ct], start=True, stop=True
                          ).then_inc(l_ready, 1)
                pe.wait_ge(kh_evac, 8 * h + c)
                pe.transpose(s_ps[:, P * (c % 4):P * (c % 4) + P], fbuf[:, p % 2, 7, cols], ident[:, :]
                             ).then_inc(kh_ready, 1)

            for s in range(2 * TB):
                k, xh = s // 2, s % 2
                if xh == 0:
                    pe.wait_ge(lo_done, B0 + TB * h + k + 1)
                pe.wait_ge(st_evac, base + s - 1)
                stream(banks[xh], k, act_hi, act_lo, xh).then_inc(st_ready, 1)
                if s in after_a:
                    pe.wait_ge(*after_a[s])
                if not tail and s == 4:
                    pe.wait_ge(t2_evac, 8 * H)
                for kind, j, jh in jobs_b(s, h, tail):
                    if kind == "z":
                        pe_z(j)
                    elif kind == "v":
                        pe_v(j)
                    elif kind == "l":
                        pe_l(j)
                    else:
                        (pe_m if kind == "m" else pe_t)(jh, j)

        def pe_m(h, c, ps=ok_ps, other=0):
            n = 8 * h + c
            p, cols = c // 2, slice(P * (c % 2), P * (c % 2) + P)
            pe.wait_ge(att_done, n + 1)
            pe.wait_ge(kh_evac, n + 1)
            pe.wait_ge(vb_evac, 4 * h + 3 + c // 4)
            pe.wait_ge(obn_done, n - other)
            pe.wait_ge(state_done, n)
            pe.matmul(ps[:, 0:DV], att[:, c, :], vtok[:, c, :], start=True, stop=(c == 0))
            if c:
                pe.matmul(ps[:, 0:DV], qh[:, P * c:P * c + P], state[:, c % 2, :], start=False, stop=True)
            pe.matmul(ps[:, DV:2 * DV], khat[:, c, :], vtok[:, c, :], start=True, stop=True
                      ).then_inc(kv_ready, 1)

        def pe_t(h, c):
            pe.wait_ge(obn_done, 8 * h + c + 1)
            pe.wait_ge(obt_evac, 8 * h + c)
            pe.wait_ge(vb_evac, 4 * h + 4)
            for e in range(2):
                mm = pe.transpose(bank3[:, P * e:P * e + P], obn[:, c % 2, P * e:P * e + P], ident[:, :])
            mm.then_inc(obt_ready, 1)

        pe_head(0, False)
        with pe.Fori(1, H) as h:
            pe_head(h, True)
        for c in range(4, 8):
            pe_m(H - 1, c, rest_ps(c), 1 if c > 4 else 0)
            if c == 7:
                pe.wait_ge(st_evac, 2 * B0 + 2 * TB * H)
                pe.wait_ge(stage_lo, H)
                pe.wait_ge(lo_done, C0 + 1)
                stream(banks[0], 0, oa_hi, oa_lo, 0, H).then_inc(mix_ready, 1)
            pe_t(H - 1, c - 1)
        pe_t(H - 1, 7)
        leave_phase(pe)

        def pair(it, n0, src_a, src_b, kts_a, first=False):
            for k in range(4):
                f = k // 2
                pe.wait_ge(lo_done, n0 + k + 1)
                for xh in range(2):
                    if kts_a == NK and k == 0 and xh == 1:
                        pe.wait_ge(nt_lo, 32)
                    w = 2 * f + xh
                    if first and k == 0 and xh == 0:
                        continue
                    if k % 2 == 0:
                        pe.wait_ge(y_done, 4 * it + (w - 1 if w >= 2 else 0))
                        stream(banks[xh], k, *src_a, xh, kts_a).then_inc(mix_ready, 1)
                    else:
                        stream(banks[2 + xh], k, *src_b, xh, staged=H if first and k == 1 and xh == 0 else 0
                               ).then_inc(mix_ready, 1)
            pe.wait_ge(lo_done, n0 + TC)
            for d in range(16):
                tt, nh = d // 2, d % 2
                if d % 8 == 0:
                    pe.wait_ge(ylo_done, 4 * it + 3 + d // 8)
                pe.wait_ge(acc_done, 16 * it + (d - 3 if d >= 4 else 0))
                cols = slice(P * tt, P * tt + P)
                for kt in range(2):
                    out = slice(HALF * nh, HALF * nh + HALF)
                    mm = three(banks[4 + d % 4], y_hi[:, kt, cols], y_lo[:, kt, cols],
                               w_hi[:, slot_of(4 + kt), out], w_lo[:, slot_of(4 + kt), out], kt == 0, kt == 1)
                mm.then_inc(down_ready, 1)

        pe.wait_ge(l_mask, 16 * H)
        pair(0, C0, (oa_hi, oa_lo), (act_hi, act_lo), H, first=True)
        with pe.Fori(1, NC_IT) as i:
            pair(i, C0 + TC * i, (oa_hi, oa_lo), (act_hi, act_lo), H)
        norm_turn(1, xn)
        pe.wait_ge(nt_lo, 16 + 9)
        with pe.Fori(0, ND_IT) as i:
            pair(NC_IT + i, D0 + TC * i, (act_hi, act_lo), (act_hi, act_lo), NK)

    ctx.close()


_INS = ["x", "positions", "norm1", "w_in", "qn_a", "kn_a", "w_a_up", "b_a", "gn_b", "w_proj_a", "w_proj_b",
        "w_out", "norm2", "w_ffn_gate", "w_ffn_up", "w_ffn_down"]


def kernel(**inputs):
    import numpy as np
    import concourse.bacc as bacc
    from concourse.bass_utils import run_bass_kernel_spmd

    nc = bacc.Bacc("TRN2", target_bir_lowering=False, num_devices=1)
    arrays = {f"in_{n}": np.ascontiguousarray(inputs[n]) for n in _INS}
    arrays["in_inv_freq"] = (10000.0 ** (-np.arange(0, 128, 2) / 128)).astype(np.float32)
    args = [nc.dram_tensor(n, a.shape, mybir.dt.from_np(a.dtype), kind="ExternalInput").ap()
            for n, a in arrays.items()]
    out = nc.dram_tensor("out_y", inputs["x"].shape, F32, kind="ExternalOutput").ap()
    decoder_layer(nc, *args, out)
    r = run_bass_kernel_spmd(nc, [arrays], core_ids=[0])
    return r.results[0]["out_y"]
```
